# Optimizing a Trainium2 kernel written in Bass

```python
import math
import jax, jax.numpy as jnp
from jax import lax
import numpy as np

D_MODEL = 1024
BATCH = 1
SEQ = 256
DEPTH = 2
DEC_BATCH = 8
DEC_SEQ = 1
PAST_LEN = 2048
PAGE_SIZE = 128

GDN_HEADS = 4
GDN_DK = 128
GDN_DV = 128
CONV_W = 4
GDN_CHUNK = 64
ML_HEADS = 4
ML_DK = 128
ML_DV = 128
ML_CHUNK = 64
S5_GROUP = 16
S5_GROUPS = D_MODEL // S5_GROUP
S5_STATE = 64
N_EXPERTS = 16
N_EXPERT_GROUPS = 4
EXPERTS_PER_GROUP = N_EXPERTS // N_EXPERT_GROUPS
TOP_K = 2
D_FF_EXPERT = 512
DN_ALPHA = (2 * DEPTH) ** 0.25
DN_BETA = (8 * DEPTH) ** -0.25
N_AB_LAYERS = (DEPTH + 1) // 2
N_S5_LAYERS = DEPTH // 2
LN_EPS = 1e-5
RMS_EPS = 1e-6
NEG_BIG = -1e30
A_QK = GDN_HEADS * GDN_DK
A_VW = GDN_HEADS * GDN_DV
A_CONV = 2 * A_QK + A_VW
B_QK = ML_HEADS * ML_DK
B_VW = ML_HEADS * ML_DV
MIX_WIDTH = A_VW + B_VW
IN_SPLITS = (A_CONV, GDN_HEADS, GDN_HEADS, A_VW, B_QK, B_QK, B_VW, ML_HEADS, ML_HEADS, B_VW)
D_IN = A_CONV + 2 * GDN_HEADS + A_VW + 2 * B_QK + 2 * B_VW + 2 * ML_HEADS

kernel_name = 'hybrid_gdn_mlstm_s5_moe_decode_step'

F32 = jnp.float32

def _layer_norm(x, g, b):
    xf = x.astype(F32)
    mu = jnp.mean(xf, -1, keepdims=True)
    var = jnp.mean(jnp.square(xf - mu), -1, keepdims=True)
    return ((xf - mu) * lax.rsqrt(var + LN_EPS) * g.astype(F32) + b.astype(F32)).astype(x.dtype)

def _rms_heads(x, w):
    return x * lax.rsqrt(jnp.mean(jnp.square(x), -1, keepdims=True) + RMS_EPS) * w.astype(F32)

def _l2norm(x):
    return x * lax.rsqrt(jnp.sum(jnp.square(x), -1, keepdims=True) + RMS_EPS)

def _pad_time(t, pad, value=0.0):
    return jnp.pad(t, [(0, 0), (0, pad)] + [(0, 0)] * (t.ndim - 2), constant_values=value)

def _to_chunks(t, n, c):
    bt = t.shape[0]
    t = t.reshape((bt, n, c) + t.shape[2:])
    return t.transpose((1, 0, 3, 2) + tuple(range(4, t.ndim)))

def _from_chunks(t, length):
    n, bt, h, c, d = t.shape
    return t.transpose((1, 0, 3, 2, 4)).reshape(bt, n * c, h, d)[:, :length]

def gated_delta_chunked(q, k, v, g, beta, S0):
    length = q.shape[1]
    c = min(GDN_CHUNK, length)
    pad = (-length) % c
    if pad:
        q, k, v, g, beta = (_pad_time(t, pad) for t in (q, k, v, g, beta))
    n = (length + pad) // c
    qc, kc, vc = (_to_chunks(t, n, c) for t in (q, k, v))
    gc, bc = (_to_chunks(t, n, c) for t in (g, beta))
    G = jnp.cumsum(gc, axis=-1)
    incl = jnp.tril(jnp.ones((c, c), bool))
    strict = jnp.tril(jnp.ones((c, c), bool), -1)
    decay = jnp.where(incl, jnp.exp(jnp.where(incl, G[..., :, None] - G[..., None, :], 0.0)), 0.0)
    kb = kc * bc[..., None]
    vb = vc * bc[..., None]
    a_low = jnp.where(strict, jnp.einsum('nbhik,nbhjk->nbhij', kb, kc) * decay, 0.0)
    m = a_low + jnp.eye(c, dtype=F32)
    u = lax.linalg.triangular_solve(m, vb, left_side=True, lower=True, unit_diagonal=True)
    w = lax.linalg.triangular_solve(m, kb * jnp.exp(G)[..., None], left_side=True, lower=True, unit_diagonal=True)
    attn = jnp.einsum('nbhik,nbhjk->nbhij', qc, kc) * decay
    q_dec = qc * jnp.exp(G)[..., None]
    k_tail = kc * jnp.exp(G[..., -1:] - G)[..., None]
    chunk_dec = jnp.exp(G[..., -1])

    def step(S, xs):
        qd, wi, ui, ai, kt, cd = xs
        v_new = ui - jnp.einsum('bhck,bhkv->bhcv', wi, S)
        o = jnp.einsum('bhck,bhkv->bhcv', qd, S) + jnp.einsum('bhij,bhjv->bhiv', ai, v_new)
        S = S * cd[..., None, None] + jnp.einsum('bhck,bhcv->bhkv', kt, v_new)
        return S, o

    S_fin, o = lax.scan(step, S0, (q_dec, w, u, attn, k_tail, chunk_dec))
    return _from_chunks(o, length), S_fin

def mlstm_chunked(q, k, v, i_pre, logf, C0, n0, m0):
    length = q.shape[1]
    c = min(ML_CHUNK, length)
    pad = (-length) % c
    if pad:
        q, k, v, logf = (_pad_time(t, pad) for t in (q, k, v, logf))
        i_pre = _pad_time(i_pre, pad, NEG_BIG)
    n = (length + pad) // c
    qc, kc, vc = (_to_chunks(t, n, c) for t in (q, k, v))
    ic, fc = (_to_chunks(t, n, c) for t in (i_pre, logf))
    b = jnp.cumsum(fc, axis=-1)
    incl = jnp.tril(jnp.ones((c, c), bool))
    dlog = jnp.where(incl, b[..., :, None] - b[..., None, :] + ic[..., None, :], NEG_BIG)
    dmax = jnp.max(dlog, axis=-1)
    qk = jnp.einsum('nbhik,nbhjk->nbhij', qc, kc)
    b_last = b[..., -1]
    tail = b_last[..., None] - b + ic

    def step(carry, xs):
        C, nv, m = carry
        qi, ki, vi, bi, dl, dm, qki, bl, tl = xs
        inter = bi + m[..., None]
        mt = jnp.maximum(inter, dm)
        wts = jnp.exp(dl - mt[..., None]) * qki
        sc = jnp.exp(inter - mt)
        num = sc[..., None] * jnp.einsum('bhck,bhkv->bhcv', qi, C) + jnp.einsum('bhij,bhjv->bhiv', wts, vi)
        den = sc * jnp.einsum('bhck,bhk->bhc', qi, nv) + jnp.sum(wts, axis=-1)
        h = num / jnp.maximum(jnp.abs(den), jnp.exp(-mt))[..., None]
        m_new = mt[..., -1]
        sd = jnp.exp(bl + m - m_new)
        wk = jnp.exp(tl - m_new[..., None])
        C = sd[..., None, None] * C + jnp.einsum('bhc,bhck,bhcv->bhkv', wk, ki, vi)
        nv = sd[..., None] * nv + jnp.einsum('bhc,bhck->bhk', wk, ki)
        return (C, nv, m_new), h

    (C_fin, n_fin, m_fin), h = lax.scan(step, (C0, n0, m0), (qc, kc, vc, b, dlog, dmax, qk, b_last, tail))
    return _from_chunks(h, length), C_fin, n_fin, m_fin

def ab_mixer(h, conv_buf, S0, C0, n0, m0, w_in, conv_w, A_log, dt_bias, gdn_norm_w,
             b_i, b_f, ml_norm_w, w_out):
    bt, length, _ = h.shape
    proj = h @ w_in
    cuts = np.cumsum(IN_SPLITS)[:-1].tolist()
    qkv_a, a_a, beta_a, z_a, q_b, k_b, v_b, i_b, f_b, o_b = jnp.split(proj, cuts, axis=-1)
    xpad = jnp.concatenate([conv_buf.astype(proj.dtype), qkv_a], axis=1)
    conv = xpad[:, :length] * conv_w[0]
    for w in range(1, CONV_W):
        conv = conv + xpad[:, w:w + length] * conv_w[w]
    new_buf = xpad[:, length:]
    conv = jax.nn.silu(conv.astype(F32))
    qa, ka, va = jnp.split(conv, [A_QK, 2 * A_QK], axis=-1)
    qa = _l2norm(qa.reshape(bt, length, GDN_HEADS, GDN_DK)) * GDN_DK ** -0.5
    ka = _l2norm(ka.reshape(bt, length, GDN_HEADS, GDN_DK))
    va = va.reshape(bt, length, GDN_HEADS, GDN_DV)
    beta = jax.nn.sigmoid(beta_a.astype(F32))
    g = -jnp.exp(A_log.astype(F32)) * jax.nn.softplus(a_a.astype(F32) + dt_bias.astype(F32))
    o_a, S_new = gated_delta_chunked(qa, ka, va, g, beta, S0.astype(F32))
    o_a = _rms_heads(o_a, gdn_norm_w) * jax.nn.silu(z_a.astype(F32).reshape(bt, length, GDN_HEADS, GDN_DV))
    qb = q_b.astype(F32).reshape(bt, length, ML_HEADS, ML_DK)
    kb = k_b.astype(F32).reshape(bt, length, ML_HEADS, ML_DK) * ML_DK ** -0.5
    vb = v_b.astype(F32).reshape(bt, length, ML_HEADS, ML_DV)
    i_pre = i_b.astype(F32) + b_i.astype(F32)
    logf = jax.nn.log_sigmoid(f_b.astype(F32) + b_f.astype(F32))
    h_b, C_new, n_new, m_new = mlstm_chunked(qb, kb, vb, i_pre, logf, C0.astype(F32), n0.astype(F32), m0.astype(F32))
    o_bh = _rms_heads(h_b, ml_norm_w) * jax.nn.sigmoid(o_b.astype(F32).reshape(bt, length, ML_HEADS, ML_DV))
    merged = jnp.concatenate([o_a.reshape(bt, length, A_VW), o_bh.reshape(bt, length, B_VW)], axis=-1).astype(h.dtype)
    return merged @ w_out, new_buf, S_new, C_new, n_new, m_new

def s5_mixer(x, h0_re, h0_im, A_re, A_im, log_dt, B_re, B_im, C_re, C_im, D_skip, w_glu_a, w_glu_b):
    bt, length, _ = x.shape
    u = x.astype(F32).reshape(bt, length, S5_GROUPS, S5_GROUP)
    a_r = A_re.astype(F32)
    a_i = A_im.astype(F32)
    dt = jnp.exp(log_dt.astype(F32))[:, None]
    mag = jnp.exp(dt * a_r)
    ab_re = mag * jnp.cos(dt * a_i)
    ab_im = mag * jnp.sin(dt * a_i)
    den = jnp.square(a_r) + jnp.square(a_i)
    nr = ab_re - 1.0
    z_re = (nr * a_r + ab_im * a_i) / den
    z_im = (ab_im * a_r - nr * a_i) / den
    br = B_re.astype(F32)
    bi = B_im.astype(F32)
    bb_re = z_re[..., None] * br - z_im[..., None] * bi
    bb_im = z_re[..., None] * bi + z_im[..., None] * br
    bu_re = jnp.einsum('blgc,gpc->blgp', u, bb_re)
    bu_im = jnp.einsum('blgc,gpc->blgp', u, bb_im)
    h0r = h0_re.astype(F32)
    h0i = h0_im.astype(F32)
    bu_re = bu_re.at[:, 0].add(ab_re * h0r - ab_im * h0i)
    bu_im = bu_im.at[:, 0].add(ab_re * h0i + ab_im * h0r)
    a_re_b = jnp.broadcast_to(ab_re, bu_re.shape)
    a_im_b = jnp.broadcast_to(ab_im, bu_im.shape)

    def combine(e1, e2):
        a1r, a1i, b1r, b1i = e1
        a2r, a2i, b2r, b2i = e2
        return (a2r * a1r - a2i * a1i, a2r * a1i + a2i * a1r,
                a2r * b1r - a2i * b1i + b2r, a2r * b1i + a2i * b1r + b2i)

    _, _, hr, hi = lax.associative_scan(combine, (a_re_b, a_im_b, bu_re, bu_im), axis=1)
    y = (jnp.einsum('blgp,gcp->blgc', hr, C_re.astype(F32)) - jnp.einsum('blgp,gcp->blgc', hi, C_im.astype(F32))
         + D_skip.astype(F32).reshape(S5_GROUPS, S5_GROUP) * u)
    gy = jax.nn.gelu(y.reshape(bt, length, D_MODEL)).astype(x.dtype)
    out = (gy @ w_glu_a) * jax.nn.sigmoid(gy @ w_glu_b)
    return out, hr[:, -1], hi[:, -1]

def moe(x, router_w, router_b, w_gate, w_up, w_down):
    logits = jnp.einsum('bld,de->ble', x.astype(F32), router_w.astype(F32))
    probs = jax.nn.softmax(logits, axis=-1)
    sel = probs + router_b.astype(F32)
    grp = sel.reshape(sel.shape[:-1] + (N_EXPERT_GROUPS, EXPERTS_PER_GROUP))
    grp_score = jnp.sum(lax.top_k(grp, TOP_K)[0], axis=-1)
    best = jnp.argmax(grp_score, axis=-1)
    in_grp = (jnp.arange(N_EXPERTS) // EXPERTS_PER_GROUP) == best[..., None]
    _, idx = lax.top_k(jnp.where(in_grp, sel, -jnp.inf), TOP_K)
    wts = jnp.take_along_axis(probs, idx, axis=-1)
    wts = wts / jnp.sum(wts, axis=-1, keepdims=True)
    comb = jnp.sum(jax.nn.one_hot(idx, N_EXPERTS, dtype=F32) * wts[..., None], axis=-2)
    hid = jax.nn.silu(jnp.einsum('bld,edf->blef', x, w_gate)) * jnp.einsum('bld,edf->blef', x, w_up)
    hid = hid * comb[..., None].astype(hid.dtype)
    return jnp.einsum('blef,efd->bld', hid, w_down)

def _trunk(x, st_conv, st_S, st_C, st_n, st_m, st_re, st_im, p):
    h = x
    l_conv, l_S, l_C, l_n, l_m, l_re, l_im = [], [], [], [], [], [], []
    for layer in range(DEPTH):
        j = layer // 2
        if layer % 2 == 0:
            mix, c_new, s_new, cm_new, n_new, m_new = ab_mixer(
                h, st_conv[:, j], st_S[:, j], st_C[:, j], st_n[:, j], st_m[:, j],
                p['w_in'][j], p['gdn_conv_w'][j], p['gdn_A_log'][j], p['gdn_dt_bias'][j], p['gdn_norm_w'][j],
                p['ml_b_i'][j], p['ml_b_f'][j], p['ml_norm_w'][j], p['w_out'][j])
            l_conv.append(c_new)
            l_S.append(s_new)
            l_C.append(cm_new)
            l_n.append(n_new)
            l_m.append(m_new)
        else:
            mix, re_new, im_new = s5_mixer(
                h, st_re[:, j], st_im[:, j], p['s5_A_re'][j], p['s5_A_im'][j], p['s5_log_dt'][j],
                p['s5_B_re'][j], p['s5_B_im'][j], p['s5_C_re'][j], p['s5_C_im'][j], p['s5_D'][j],
                p['s5_w_glu_a'][j], p['s5_w_glu_b'][j])
            l_re.append(re_new)
            l_im.append(im_new)
        h = _layer_norm(DN_ALPHA * h + mix, p['ln_mix_g'][layer], p['ln_mix_b'][layer])
        ffn = moe(h, p['router_w'], p['router_b'], p['moe_w_gate'][layer], p['moe_w_up'][layer], p['moe_w_down'][layer])
        h = _layer_norm(DN_ALPHA * h + ffn, p['ln_ffn_g'][layer], p['ln_ffn_b'][layer])
    stk = lambda lst, ref: jnp.stack(lst, axis=1).astype(ref.dtype)
    return (h, stk(l_conv, st_conv), stk(l_S, st_S), stk(l_C, st_C), stk(l_n, st_n), stk(l_m, st_m),
            stk(l_re, st_re), stk(l_im, st_im))

def setup_inputs(seed: int = 0) -> dict:
    key = jax.random.key(seed)
    ks = iter(jax.random.split(key, 64))
    nrm = lambda shape, scale=1.0: jax.random.normal(next(ks), shape, F32) * scale
    uni = lambda shape, lo, hi: jax.random.uniform(next(ks), shape, F32, lo, hi)
    na, ns = N_AB_LAYERS, N_S5_LAYERS
    gdn_dt = jnp.exp(uni((na, GDN_HEADS), math.log(1e-3), math.log(1e-1)))
    s5_a_im = math.pi * jnp.broadcast_to(jnp.arange(S5_STATE, dtype=F32), (ns, S5_GROUPS, S5_STATE))
    return {
        'x_prompt': nrm((BATCH, SEQ, D_MODEL)),
        'x_sample': nrm((DEC_BATCH, DEC_SEQ, D_MODEL)),
        'state_gdn_conv': nrm((DEC_BATCH, na, CONV_W - 1, A_CONV)),
        'state_gdn_S': nrm((DEC_BATCH, na, GDN_HEADS, GDN_DK, GDN_DV), 0.1),
        'state_mlstm_C': nrm((DEC_BATCH, na, ML_HEADS, ML_DK, ML_DV), 0.1),
        'state_mlstm_n': nrm((DEC_BATCH, na, ML_HEADS, ML_DK), 0.1),
        'state_mlstm_m': 1.0 + nrm((DEC_BATCH, na, ML_HEADS), 0.5),
        'state_s5_re': nrm((DEC_BATCH, ns, S5_GROUPS, S5_STATE), 0.5),
        'state_s5_im': nrm((DEC_BATCH, ns, S5_GROUPS, S5_STATE), 0.5),
        'w_in': nrm((na, D_MODEL, D_IN), D_MODEL ** -0.5),
        'gdn_conv_w': nrm((na, CONV_W, A_CONV), CONV_W ** -0.5),
        'gdn_A_log': jnp.log(uni((na, GDN_HEADS), 1.0, 16.0)),
        'gdn_dt_bias': jnp.log(jnp.expm1(gdn_dt)),
        'gdn_norm_w': 1.0 + nrm((na, GDN_DV), 0.02),
        'ml_b_i': nrm((na, ML_HEADS), 0.1),
        'ml_b_f': uni((na, ML_HEADS), 3.0, 6.0),
        'ml_norm_w': 1.0 + nrm((na, ML_DV), 0.02),
        'w_out': nrm((na, MIX_WIDTH, D_MODEL), MIX_WIDTH ** -0.5 * DN_BETA),
        's5_A_re': -0.5 * jnp.exp(nrm((ns, S5_GROUPS, S5_STATE), 0.02)),
        's5_A_im': s5_a_im + nrm((ns, S5_GROUPS, S5_STATE), 0.01),
        's5_log_dt': uni((ns, S5_GROUPS), math.log(1e-3), math.log(1e-1)),
        's5_B_re': nrm((ns, S5_GROUPS, S5_STATE, S5_GROUP), (2 * S5_GROUP) ** -0.5),
        's5_B_im': nrm((ns, S5_GROUPS, S5_STATE, S5_GROUP), (2 * S5_GROUP) ** -0.5),
        's5_C_re': nrm((ns, S5_GROUPS, S5_GROUP, S5_STATE), (2 * S5_STATE) ** -0.5),
        's5_C_im': nrm((ns, S5_GROUPS, S5_GROUP, S5_STATE), (2 * S5_STATE) ** -0.5),
        's5_D': nrm((ns, D_MODEL)),
        's5_w_glu_a': nrm((ns, D_MODEL, D_MODEL), D_MODEL ** -0.5 * DN_BETA),
        's5_w_glu_b': nrm((ns, D_MODEL, D_MODEL), D_MODEL ** -0.5),
        'router_w': nrm((D_MODEL, N_EXPERTS), D_MODEL ** -0.5),
        'router_b': nrm((N_EXPERTS,), 0.01),
        'moe_w_gate': nrm((DEPTH, N_EXPERTS, D_MODEL, D_FF_EXPERT), D_MODEL ** -0.5),
        'moe_w_up': nrm((DEPTH, N_EXPERTS, D_MODEL, D_FF_EXPERT), D_MODEL ** -0.5),
        'moe_w_down': nrm((DEPTH, N_EXPERTS, D_FF_EXPERT, D_MODEL), D_FF_EXPERT ** -0.5 * DN_BETA),
        'ln_mix_g': 1.0 + nrm((DEPTH, D_MODEL), 0.02),
        'ln_mix_b': nrm((DEPTH, D_MODEL), 0.02),
        'ln_ffn_g': 1.0 + nrm((DEPTH, D_MODEL), 0.02),
        'ln_ffn_b': nrm((DEPTH, D_MODEL), 0.02),
    }

def reference(x_prompt, x_sample, state_gdn_conv, state_gdn_S, state_mlstm_C, state_mlstm_n, state_mlstm_m,
              state_s5_re, state_s5_im, w_in, gdn_conv_w, gdn_A_log, gdn_dt_bias, gdn_norm_w, ml_b_i, ml_b_f,
              ml_norm_w, w_out, s5_A_re, s5_A_im, s5_log_dt, s5_B_re, s5_B_im, s5_C_re, s5_C_im, s5_D,
              s5_w_glu_a, s5_w_glu_b, router_w, router_b, moe_w_gate, moe_w_up, moe_w_down,
              ln_mix_g, ln_mix_b, ln_ffn_g, ln_ffn_b):
    params = dict(w_in=w_in, gdn_conv_w=gdn_conv_w, gdn_A_log=gdn_A_log, gdn_dt_bias=gdn_dt_bias,
                  gdn_norm_w=gdn_norm_w, ml_b_i=ml_b_i, ml_b_f=ml_b_f, ml_norm_w=ml_norm_w, w_out=w_out,
                  s5_A_re=s5_A_re, s5_A_im=s5_A_im, s5_log_dt=s5_log_dt, s5_B_re=s5_B_re, s5_B_im=s5_B_im,
                  s5_C_re=s5_C_re, s5_C_im=s5_C_im, s5_D=s5_D, s5_w_glu_a=s5_w_glu_a, s5_w_glu_b=s5_w_glu_b,
                  router_w=router_w, router_b=router_b, moe_w_gate=moe_w_gate, moe_w_up=moe_w_up,
                  moe_w_down=moe_w_down, ln_mix_g=ln_mix_g, ln_mix_b=ln_mix_b, ln_ffn_g=ln_ffn_g, ln_ffn_b=ln_ffn_b)
    bp = x_prompt.shape[0]
    dt = x_prompt.dtype
    z_conv = jnp.zeros((bp, N_AB_LAYERS, CONV_W - 1, A_CONV), dt)
    z_S = jnp.zeros((bp, N_AB_LAYERS, GDN_HEADS, GDN_DK, GDN_DV), dt)
    z_C = jnp.zeros((bp, N_AB_LAYERS, ML_HEADS, ML_DK, ML_DV), dt)
    z_n = jnp.zeros((bp, N_AB_LAYERS, ML_HEADS, ML_DK), dt)
    z_m = jnp.zeros((bp, N_AB_LAYERS, ML_HEADS), dt)
    z_re = jnp.zeros((bp, N_S5_LAYERS, S5_GROUPS, S5_STATE), dt)
    z_im = jnp.zeros((bp, N_S5_LAYERS, S5_GROUPS, S5_STATE), dt)
    y_prompt, p_conv, p_S, p_C, p_n, p_m, p_re, p_im = _trunk(
        x_prompt, z_conv, z_S, z_C, z_n, z_m, z_re, z_im, params)
    y_sample, s_conv, s_S, s_C, s_n, s_m, s_re, s_im = _trunk(
        x_sample, state_gdn_conv, state_gdn_S, state_mlstm_C, state_mlstm_n, state_mlstm_m,
        state_s5_re, state_s5_im, params)
    return (y_prompt, y_sample, p_conv, p_S, p_C, p_n, p_m, p_re, p_im,
            s_conv, s_S, s_C, s_n, s_m, s_re, s_im)


_drawn_inputs = setup_inputs


def setup_inputs(seed=0):
    import zlib

    import numpy as np

    out = dict(_drawn_inputs(seed))
    spreads = {}
    factors = {'ml_norm_w': 8.934, 's5_A_re': 16.504, 'gdn_norm_w': 3.618}
    for name, (base, spread) in spreads.items():
        noise = np.random.default_rng([zlib.crc32(name.encode()), seed]).standard_normal(out[name].shape)
        drawn = base * np.exp(spread * noise) if base else spread * noise
        out[name] = __import__('jax').numpy.asarray(drawn.astype(out[name].dtype))
    for name, factor in factors.items():
        out[name] = (out[name] * factor).astype(out[name].dtype)
    return out
```

```python
from contextlib import ExitStack

import numpy as np

import concourse.bass as bass
from concourse import mybir
from concourse.alu_op_type import AluOpType as ALU

F32 = mybir.dt.float32
I32 = mybir.dt.int32
U32 = mybir.dt.uint32
ACT = mybir.ActivationFunctionType
AX = mybir.AxisListType.X

P = 128
D = 1024
DC = D // P
SEQ, NS = 256, 8
T = SEQ + NS
TT = SEQ // P
H, DK = 4, 128
CONV = 3 * H * DK
CW = 4
D_IN = CONV + 2 * H + 4 * H * DK + H * DK + 2 * H
Z0 = CONV + 2 * H
IF0 = Z0 + 4 * H * DK
O0 = IF0 + 2 * H
HS = H * NS
G5, C5, N5 = 64, 16, 64
PT = G5 // 2
NE, NG, EPG, FF = 16, 4, 4, 512
SLOT = 64
ROUNDS = (T + SLOT - 1) // SLOT
LISTS = NE * ROUNDS
NOWHERE = 1 << 20
ALPHA = 4.0 ** 0.25
LN_EPS, RMS_EPS = 1e-5, 1e-6
QSCALE = DK ** -0.5


class Steps:

    def __init__(self, sem, book, engine):
        self.sem, self.engine, self.count = sem, engine, 0
        self.known, self.book = book["known"], book["new"]

    def done(self, name=None):
        self.count += 1
        if name is not None:
            self.book[self.engine, name] = self.count
        return self.sem, 1

    def at(self, name):
        if self.known and (self.engine, name) not in self.known:
            raise KeyError(f"{self.engine} has no step {name}")
        return self.sem, self.known.get((self.engine, name), 1)

    def last(self):
        return self.sem, max(self.count, 1)


def carve(region, base, **sizes):
    at, out = base, {}
    for name, size in sizes.items():
        out[name] = at
        at += size
    out["end"] = at
    return out


def build(nc, io, out, book):
    ctx = ExitStack()
    with ctx:
        ctx.enter_context(nc.allow_non_contiguous_dma(reason="a few dozen gate values"))
        sems = {}

        def sem(name):
            if name not in sems:
                sems[name] = ctx.enter_context(nc.semaphore(name))
            return sems[name]

        pe, dv, ac, po = (Steps(sem(f"{n}_steps"), book, n) for n in ("pe", "dve", "act", "pool"))

        ring = ctx.enter_context(nc.sbuf_tensor("ring", [P, 2 * 8192 + 2 * 4096], F32))
        WORK = 26596
        work = ctx.enter_context(nc.sbuf_tensor("work", [P, WORK], F32))
        ps = ctx.enter_context(nc.psum_tensor("ps", [P, 8, 512], F32))

        def view(region, at, *shape):
            size = int(np.prod(shape))
            v = region[:, at:at + size]
            if len(shape) > 1:
                names = "abcde"[:len(shape)]
                v = v.rearrange(f"p ({' '.join(names)}) -> p {' '.join(names)}",
                                **dict(zip(names, shape)))
            return v

        gate_w = [view(ring, s * 8192, DC, FF) for s in range(2)]
        up_w = [view(ring, s * 8192 + 4096, DC, FF) for s in range(2)]
        down_w = [view(ring, 16384 + s * 4096, 4, D) for s in range(2)]

        def dram(name, shape, dtype=F32):
            return nc.dram_tensor(name, shape, dtype, kind="Internal").ap()

        def tok(t):
            return P if t < TT else NS

        C0 = carve(None, 0, ident=P, ones=P, upper=P, levels=7 * P, heads=64, cols=16)
        const = ctx.enter_context(nc.sbuf_tensor("const", [P, C0["end"]], F32))
        ident = view(const, C0["ident"], P)
        ones = view(const, C0["ones"], P)
        upper = view(const, C0["upper"], P)
        level = view(const, C0["levels"], 7, P)
        head_col = view(const, C0["heads"], 8, 8)
        eps_rms, eps_ln = (const[:, C0["cols"] + i:C0["cols"] + i + 1] for i in range(2))

        def row_of(h, rows=H):
            return ident[0:rows, h:h + 1].to_broadcast([rows, P])

        A = carve(work, 0, xT=DC * T, raw=12 * (CW - 1 + T), cv=12 * T, pj=20 * T, rows=14 * T,
                  negwT=512, vnew=512, s1=512, qdec=512, oT=8 * T, convT=12 * 28, gatew=0,
                  params=P, paramsT=64, cols=64, gp=16, kq=64, sb=H * 40, small=12 * HS,
                  krow=4 * P, vblk=1024, nrow=P, sr=40, cd=H)
        assert A["end"] <= WORK, A["end"]
        xT = view(work, A["xT"], DC, T)
        raw = view(work, A["raw"], 12, CW - 1 + T)
        cv = view(work, A["cv"], 12, T)
        pj = view(work, A["pj"], 20, T)
        Z_, QB, KB, VB, OB = 0, 4, 8, 12, 16
        R = view(work, A["rows"], 14, T)
        tokA = A["raw"]
        kbg, vb, ktail = (view(work, tokA + i * 1024, 8, P) for i in range(3))
        kwk, vm = kbg, vb
        sq = view(work, tokA, 8, T)
        negwT, vnew, s1, qdec = (view(work, A[n], H, P) for n in ("negwT", "vnew", "s1", "qdec"))
        oT = view(work, A["oT"], 8, T)
        cs_in = view(work, A["oT"], CONV)
        convT = view(work, A["convT"], 12, 28)
        params = view(work, A["params"], P)
        paramsT = view(work, A["paramsT"], 64)
        cols = view(work, A["cols"], 6, TT, H)
        gp = view(work, A["gp"], 16)
        kq = view(work, A["kq"], 2, HS)
        sb = view(work, A["sb"], H, 5, NS)
        small = view(work, A["small"], 12, HS)
        krow = view(work, A["krow"], 4, P)
        vblk = [view(work, A["vblk"] + i * 512, 4, P) for i in range(2)]
        sr = view(work, A["sr"], 5, NS)
        cd = view(work, A["cd"], H)
        nrow = view(work, A["nrow"], P)
        crow = view(work, A["vnew"], 3, 12, NS)
        win = [view(ring, s, DC, 512) for s in (0, 4096, 16384, 20480)]
        wout = view(ring, 0, DC, D)
        Sst = view(ring, 8192, HS, P)
        Cst = view(ring, 12288, HS, P)
        tinv, tinvT, at_l, at_f, zz, dec, attnT = (view(ring, 16384 + i * 1024, 8, P) for i in range(7))
        NEG_G, BETA, BETA_EG, TAIL_A, I_F, TAIL_B = range(6)
        EG, BT, FP, IP, EM = range(5)
        wexp, wq = (view(ring, 16384 + i * 1536, H, 384) for i in range(2))
        gw = view(work, A["vnew"], DC, P)
        gwin = view(work, A["qdec"], 2, DC, 8)
        xtok = view(work, A["cv"], 3, D)
        (RA, RF, RB_, RI, RG, REG, RNG, RBG, RKT, RIF, RWK, RFM, RM, RT_) = range(14)

        x_all = [io["x_prompt"].rearrange("o (t p) d -> p (o t) d", p=P), io["x_sample"].rearrange("b o d -> (b o) d")]
        w_in = io["w_in"].rearrange("o (k p) n -> p (o k) n", p=P)
        group_at = [0, 512, 1024, Z0, Z0 + 512, Z0 + 1024, Z0 + 1536, O0]

        def ab_loads(sp):
            sp.dma_start(xtok[:, 0:TT, :], x_all[0]).then_inc(sem("x_in"), 16)
            sp.dma_start(xtok[0:NS, TT, :], x_all[1]).then_inc(sem("x_in"), 16)
            s5_param_loads(sp)
            for i, at in enumerate((CONV, IF0)):
                sp.dma_start(gwin[:, i], w_in[:, :, at:at + 8]).then_inc(sem("gates_in"), 16)
            for g in range(4):
                sp.dma_start(win[g], w_in[:, :, group_at[g]:group_at[g] + 512]).then_inc(sem(f"w_in{g}"), 16)
            s5_cols_store(sp)
            s5_tables_store(sp)
            s5_tables_stored(sp)
            for h in range(H):
                sp.dma_start(Sst[:, h * NS:(h + 1) * NS, :],
                             io["state_gdn_S"][:, 0, h].rearrange("b k v -> k b v")).then_inc(sem("states_in"), 16)
                sp.dma_start(Cst[:, h * NS:(h + 1) * NS, :],
                             io["state_mlstm_C"][:, 0, h].rearrange("b k v -> k b v")).then_inc(sem("states_in"), 16)
            sp.wait_ge(*pe.at("proj23"))
            sp.dma_start(wout, io["w_out"].rearrange("o (k p) n -> p (o k) n", p=P)).then_inc(sem("w_out"), 16)

        def ab_small_loads(q):
            q.dma_start(cs_in[0:24, :], io["state_gdn_conv"].rearrange("b o w c -> (b o w) c")).then_inc(sem("conv_in"), 16)
            q.dma_start(cs_in[24:28, :], io["gdn_conv_w"].rearrange("o w c -> (o w) c")).then_inc(sem("conv_in"), 16)
            for i, name in enumerate(("gdn_A_log", "gdn_dt_bias", "ml_b_i", "ml_b_f")):
                q.dma_start(gp[0:H, i:i + 1], io[name].rearrange("o h -> h o")).then_inc(sem("params_in"), 16)
            q.dma_start(gp[0:H, 4:4 + NS], io["state_mlstm_m"].rearrange("b o h -> h (o b)")).then_inc(sem("params_in"), 16)
            q.dma_start(params[0:1, :], io["gdn_norm_w"]).then_inc(sem("params_in"), 16)
            q.dma_start(params[1:2, :], io["ml_norm_w"]).then_inc(sem("params_in"), 16)
            for h in range(H):
                q.dma_start(params[2 + h * NS:2 + (h + 1) * NS, :],
                            io["state_mlstm_n"][:, 0, h]).then_inc(sem("params_in"), 16)
            q.dma_start(out["s_conv"][:, 0, 0:2], io["state_gdn_conv"][:, 0, 1:3]).then_inc(sem("stores"), 16)
        PARAMS_IN = 16 * (4 + 1 + 2 + H)

        def ab_consts(pool):
            nc.gpsimd.memset(ones, 1.0).then_inc(*po.done())
            nc.gpsimd.memset(ident, 0.0).then_inc(*po.done())
            nc.gpsimd.memset(gw, 0.0).then_inc(*po.done("gw_zero"))
            nc.gpsimd.memset(raw[:, :, 0:CW - 1], 0.0).then_inc(*po.done())
            nc.gpsimd.memset(head_col, 0.0).then_inc(*po.done())
            nc.gpsimd.memset(eps_rms, RMS_EPS).then_inc(*po.done())
            nc.gpsimd.memset(eps_ln, LN_EPS).then_inc(*po.done())
            pool.wait_ge(*po.last())
            nc.gpsimd.affine_select(out=ident, in_=ident, pattern=[[-1, P]], compare_op=ALU.not_equal, fill=1.0,
                                    base=0, channel_multiplier=1).then_inc(*po.done("ident"))
            nc.gpsimd.affine_select(out=upper, in_=ones, pattern=[[1, P]], compare_op=ALU.is_ge, fill=0.0,
                                    base=0, channel_multiplier=-1).then_inc(*po.done())
            nc.gpsimd.memset(head_col.rearrange("p a b -> p (a b)")[:, 0::9], 1.0).then_inc(*po.done("head_col"))
            iota_i = view(work, A["vblk"], P).bitcast(I32)
            iota_j = view(work, A["vblk"] + P, P).bitcast(I32)
            nc.gpsimd.iota(iota_i, pattern=[[1, P]], base=0, channel_multiplier=0).then_inc(*po.done())
            nc.gpsimd.iota(iota_j, pattern=[[0, P]], base=0, channel_multiplier=1).then_inc(*po.done("consts"))

        def ab_levels(dve):
            iota_i = view(work, A["vblk"], P).bitcast(I32)
            iota_j = view(work, A["vblk"] + P, P).bitcast(I32)
            xor_f = view(work, A["vblk"], P)
            dve.wait_ge(*po.at("consts"))
            nc.vector.tensor_tensor(iota_j, iota_i, iota_j, ALU.bitwise_xor).then_inc(*dv.done())
            dve.wait_ge(*dv.last())
            nc.vector.tensor_copy(xor_f, iota_j).then_inc(*dv.done())
            dve.wait_ge(*dv.last())
            nc.vector.tensor_tensor(xor_f, xor_f, upper, ALU.mult).then_inc(*dv.done())
            dve.wait_ge(*dv.last())
            for b in range(7):
                nc.vector.tensor_scalar(level[:, b], xor_f, float(2 ** b), None, ALU.is_ge).then_inc(*dv.done())
            for b in range(6):
                dve.wait_ge(*dv.last())
                nc.vector.tensor_tensor(level[:, b], level[:, b], level[:, b + 1], ALU.subtract).then_inc(*dv.done("levels"))

        def proj_bank(j):
            return 1 + j % 4

        def ab_pe_project(t):
            t.wait_ge(sem("x_in"), 32)
            t.wait_ge(*po.at("ident"))
            for k in range(DC):
                for i in range(3):
                    n = tok(i)
                    last = nc.tensor.transpose(ps[:, k, i * P:i * P + n], xtok[0:n, i, k * P:(k + 1) * P], ident[0:n, 0:n])
                last.then_inc(*pe.done(f"xT{k}"))
            t.wait_ge(*dv.at("gw"))
            t.wait_ge(*ac.at("xT"))
            t.wait_ge(*dv.at("xT"))
            for k in range(DC):
                last = nc.tensor.matmul(ps[:, 0, 0:T], gw[:, k], xT[:, k], start=k == 0, stop=k == DC - 1)
            last.then_inc(*pe.done("gates"))
            t.wait_ge(sem("conv_in"), 32)
            for c in range(12):
                last = nc.tensor.transpose(ps[:, 5, c * 28:c * 28 + 28], cs_in[0:28, c * P:(c + 1) * P], ident[0:28, 0:28])
            last.then_inc(*pe.done("convT"))
            t.wait_ge(sem("params_in"), PARAMS_IN)
            nc.tensor.transpose(ps[:, 6, 0:34], params[0:34, :], ident[0:34, 0:34]).then_inc(*pe.done("paramsT"))
            s5_param_pe(t)
            for j in range(32):
                g = j // 4
                if j % 4 == 0:
                    t.wait_ge(sem(f"w_in{g % 4}"), 16 * (1 + g // 4))
                if j >= 4:
                    t.wait_ge(*ac.at(f"proj{j - 4}"))
                if j == 10:
                    ab_pe_rows(t)
                if j == 14:
                    ab_pe_new_rows(t)
                for k in range(DC):
                    last = nc.tensor.matmul(ps[:, proj_bank(j), 0:T], win[g % 4][:, k, (j % 4) * P:(j % 4 + 1) * P],
                                            xT[:, k], start=k == 0, stop=k == DC - 1)
                last.then_inc(*pe.done(f"proj{j}"))

        def ab_pe_new_rows(t):
            t.wait_ge(*ac.at("proj11"))
            t.wait_ge(*dv.at("paramsT"))
            for c in range(12):
                last = nc.tensor.transpose(ps[0:11, 5 + c // 4, (c % 4) * P:(c % 4 + 1) * P],
                                           raw[:, c, SEQ:SEQ + 11], ident)
            last.then_inc(*pe.done("new_rows"))

        def ab_pe_rows(t):
            t.wait_ge(*dv.at("rows"))
            t.wait_ge(*ac.at("rows"))
            for n, r in enumerate((RNG, RB_, RBG, RKT, RIF, RWK)):
                for i in range(TT):
                    nc.tensor.transpose(ps[:, 0, (n * TT + i) * H:(n * TT + i + 1) * H], R[0:H, r, i * P:(i + 1) * P], ident[0:H, 0:H])
            for h in range(H):
                last = nc.tensor.matmul(ps[:, 0, 64 + 40 * h:104 + 40 * h], row_of(h), sr[0:H].rearrange("p a b -> p (a b)"),
                                        start=True, stop=True)
            last.then_inc(*pe.done("cols"))

        def ab_act_rows(a):
            a.wait_ge(sem("params_in"), PARAMS_IN)
            nc.scalar.activation(gp[0:H, 12:13], gp[0:H, 0:1], ACT.Exp).then_inc(*ac.done("exp_A"))
            a.wait_ge(*dv.at("abs_x"))
            nc.scalar.activation(R[0:H, REG:REG + 3], R[0:H, REG:REG + 3], ACT.Exp, scale=-1.0).then_inc(*ac.done())
            a.wait_ge(*ac.last())
            nc.scalar.activation(R[0:H, REG:REG + 3], R[0:H, REG:REG + 3], ACT.Ln, bias=1.0).then_inc(*ac.done("log1p"))
            a.wait_ge(*dv.at("G"))
            nc.scalar.activation(R[0:H, RB_], R[0:H, RB_], ACT.Exp).then_inc(*ac.done())
            nc.scalar.activation(R[0:H, REG], R[0:H, RT_], ACT.Exp).then_inc(*ac.done("beta"))
            nc.scalar.activation(R[0:H, RKT, 0:SEQ], R[0:H, RKT, 0:SEQ], ACT.Exp).then_inc(*ac.done())
            a.wait_ge(*dv.at("m"))
            nc.scalar.activation(R[0:H, RWK, 0:SEQ], R[0:H, RWK, 0:SEQ], ACT.Exp).then_inc(*ac.done())
            nc.scalar.activation(R[0:H, RG], R[0:H, RM], ACT.Exp, scale=-1.0).then_inc(*ac.done())
            nc.scalar.activation(sr[0:H, 2:4], sr[0:H, 2:4], ACT.Exp).then_inc(*ac.done("rows"))

        def ab_dve_rows(v):
            r = lambda i, a=0, b=T: R[0:H, i, a:b]
            one = lambda n: ones[0:H, 0:1].to_broadcast([H, n])
            v.wait_ge(sem("params_in"), PARAMS_IN)
            for row, par in ((RA, 1), (RF, 3), (RI, 2)):
                nc.vector.tensor_scalar(r(row), r(row), gp[0:H, par:par + 1], None, ALU.add).then_inc(*dv.done())
            v.wait_ge(*dv.last())
            nc.vector.scalar_tensor_tensor(R[0:H, REG:REG + 3], R[0:H, RA:RA + 3], -1.0, R[0:H, RA:RA + 3], ALU.mult, ALU.max).then_inc(*dv.done("abs_x"))
            v.wait_ge(*ac.at("log1p"))
            nc.vector.scalar_tensor_tensor(r(RG), r(RA), 0.0, r(REG), ALU.max, ALU.add).then_inc(*dv.done())
            nc.vector.scalar_tensor_tensor(r(RF), r(RF), 0.0, r(REG + 1), ALU.min, ALU.subtract).then_inc(*dv.done())
            nc.vector.scalar_tensor_tensor(r(RB_), r(RB_), 0.0, r(REG + 2), ALU.min, ALU.subtract).then_inc(*dv.done())
            v.wait_ge(*dv.last())
            nc.vector.tensor_scalar(r(RG), r(RG), gp[0:H, 12:13], -1.0, ALU.mult, ALU.mult).then_inc(*dv.done())
            v.wait_ge(*dv.last())
            for i in range(TT):
                nc.vector.tensor_tensor_scan(r(RT_, i * P, (i + 1) * P), one(P), r(RG, i * P, (i + 1) * P), 0.0, ALU.mult, ALU.add).then_inc(*dv.done())
            nc.vector.tensor_copy(r(RT_, SEQ), r(RG, SEQ)).then_inc(*dv.done())
            v.wait_ge(*dv.last())
            nc.vector.tensor_scalar(r(RNG, 0, SEQ), r(RT_, 0, SEQ), -1.0, None, ALU.mult).then_inc(*dv.done())
            for i in range(TT):
                nc.vector.tensor_scalar(r(RKT, i * P, (i + 1) * P), r(RT_, i * P, (i + 1) * P),
                                        r(RT_, i * P + P - 1, (i + 1) * P), -1.0, ALU.subtract, ALU.mult).then_inc(*dv.done("G"))
            nc.vector.tensor_tensor_scan(r(RM, 0, SEQ), r(RF, 0, SEQ), r(RI, 0, SEQ), 0.0, ALU.add, ALU.max).then_inc(*dv.done())
            nc.vector.tensor_tensor_scan(r(RG, 0, SEQ), one(SEQ), r(RF, 0, SEQ), 0.0, ALU.mult, ALU.add).then_inc(*dv.done())
            nc.vector.tensor_tensor(sr[0:H, 2], r(RF, SEQ), gp[0:H, 4:4 + NS], ALU.add).then_inc(*dv.done())
            v.wait_ge(*dv.last())
            nc.vector.tensor_tensor(r(RIF, 0, SEQ), r(RI, 0, SEQ), r(RG, 0, SEQ), ALU.subtract).then_inc(*dv.done())
            nc.vector.tensor_tensor(r(RFM, 0, SEQ), r(RG, 0, SEQ), r(RM, 0, SEQ), ALU.subtract).then_inc(*dv.done())
            nc.vector.tensor_tensor(r(RM, SEQ), sr[0:H, 2], r(RI, SEQ), ALU.max).then_inc(*dv.done())
            v.wait_ge(*dv.last())
            nc.vector.tensor_scalar(r(RWK, 0, SEQ), r(RIF, 0, SEQ), r(RFM, SEQ - 1, SEQ), None, ALU.add).then_inc(*dv.done())
            nc.vector.tensor_tensor(sr[0:H, 2], sr[0:H, 2], r(RM, SEQ), ALU.subtract).then_inc(*dv.done())
            nc.vector.tensor_tensor(sr[0:H, 3], r(RI, SEQ), r(RM, SEQ), ALU.subtract).then_inc(*dv.done("m"))
            v.wait_ge(*ac.at("beta"))
            nc.vector.tensor_tensor(r(RBG, 0, SEQ), r(RB_, 0, SEQ), r(REG, 0, SEQ), ALU.mult).then_inc(*dv.done())
            nc.vector.tensor_copy(sr[0:H, 0], r(REG, SEQ)).then_inc(*dv.done())
            nc.vector.tensor_copy(sr[0:H, 1], r(RB_, SEQ)).then_inc(*dv.done())
            v.wait_ge(*ac.at("rows"))
            nc.vector.tensor_copy(sr[0:H, 4], r(RG, SEQ)).then_inc(*dv.done("rows"))

        def next_group(a, j):
            g = j // 4 + 4
            if j % 4 == 3 and g < 8:
                a.dma_start(win[g % 4], w_in[:, :, group_at[g]:group_at[g] + 512]).then_inc(sem(f"w_in{g % 4}"), 16)

        def ab_act_project(a):
            s5_param_act0(a)
            for k in range(0, DC, 2):
                a.wait_ge(*pe.at(f"xT{k}"))
                nc.scalar.copy(xT[:, k], ps[:, k, 0:T]).then_inc(*ac.done("xT"))
            s5_param_act1(a)
            ab_act_rows(a)
            for j in range(12):
                a.wait_ge(*pe.at(f"proj{j}"))
                next_group(a, j)
                if j == 0:
                    a.wait_ge(*po.at("ident"))
                nc.scalar.copy(raw[:, j, CW - 1:], ps[:, proj_bank(j), 0:T]).then_inc(*ac.done(f"proj{j}"))
            for j in range(12, 32):
                a.wait_ge(*pe.at(f"proj{j}"))
                next_group(a, j)
                c = j - 12
                if KB <= c < VB:
                    nc.scalar.mul(pj[:, c], ps[:, proj_bank(j), 0:T], QSCALE).then_inc(*ac.done(f"proj{j}"))
                else:
                    nc.scalar.copy(pj[:, c], ps[:, proj_bank(j), 0:T]).then_inc(*ac.done(f"proj{j}"))
                if j == 15:
                    a.wait_ge(*ac.last())
                    nc.scalar.activation(pj[:, Z_:Z_ + 4], pj[:, Z_:Z_ + 4], ACT.Silu).then_inc(*ac.done("silu_z"))
                    a.wait_ge(*dv.at("conv"))
                    nc.scalar.activation(cv, cv, ACT.Silu).then_inc(*ac.done("silu_cv"))
                    a.wait_ge(*ac.last())
                    a.wait_ge(*dv.at("conv_rest"))
                    nc.scalar.activation(sq, cv[:, 0:8], ACT.Square).then_inc(*ac.done("sq_cv"))
            a.wait_ge(*ac.last())
            nc.scalar.activation(pj[:, OB:OB + 4], pj[:, OB:OB + 4], ACT.Tanh, scale=0.5).then_inc(*ac.done("tanh_o"))

        def ab_dve_project(v):
            v.wait_ge(sem("gates_in"), 32)
            v.wait_ge(*po.at("gw_zero"))
            for i in range(4):
                nc.vector.tensor_copy(gw[:, :, 32 * i:32 * i + H], gwin[:, i // 2, :, (i % 2) * H:(i % 2) * H + H]).then_inc(*dv.done("gw"))
            for k in range(1, DC, 2):
                v.wait_ge(*pe.at(f"xT{k}"))
                nc.vector.tensor_copy(xT[:, k], ps[:, k, 0:T]).then_inc(*dv.done("xT"))
            s5_param_dve(v)
            ab_levels(v)
            v.wait_ge(*pe.at("convT"))
            nc.vector.tensor_copy(convT, ps[:, 5, 0:336].rearrange("p (c n) -> p c n", c=12)).then_inc(*dv.done("convT"))
            v.wait_ge(*pe.at("paramsT"))
            nc.vector.tensor_copy(paramsT[:, 0:34], ps[:, 6, 0:34]).then_inc(*dv.done("paramsT"))
            v.wait_ge(*pe.at("gates"))
            for i, r in enumerate((RA, RB_, RI, RF)):
                nc.vector.tensor_copy(R[0:H, r], ps[32 * i:32 * i + H, 0, 0:T]).then_inc(*dv.done("gate_rows"))
            s5_cols_dve(v)
            v.wait_ge(*dv.last())
            ab_dve_rows(v)
            v.wait_ge(*pe.at("cols"))
            nc.vector.tensor_copy(cols, ps[:, 0, 0:48].rearrange("p (a b c) -> p a b c", a=6, b=TT)).then_inc(*dv.done())
            nc.vector.tensor_copy(sb, ps[:, 0, 64:224].rearrange("p (a b c) -> p a b c", a=H, b=5)).then_inc(*dv.done("cols"))
            for c in range(12):
                v.wait_ge(*ac.at(f"proj{c}"))
                y = cv[:, c, 0:SEQ]
                nc.vector.tensor_scalar(y, raw[:, c, 0:SEQ], convT[:, c, 24:25], None, ALU.mult).then_inc(*dv.done())
                for w in range(1, CW):
                    v.wait_ge(*dv.last())
                    nc.vector.scalar_tensor_tensor(y, raw[:, c, w:w + SEQ], convT[:, c, 24 + w:25 + w], y,
                                                   ALU.mult, ALU.add).then_inc(*dv.done())
            st = convT[:, :, 0:24].rearrange("p c (b w) -> p c b w", w=3)
            y = cv[:, :, SEQ:]
            nc.vector.tensor_tensor(y, raw[:, :, CW - 1 + SEQ:], convT[:, :, 27:28].to_broadcast([P, 12, NS]), ALU.mult).then_inc(*dv.done())
            for w in range(CW - 1):
                nc.vector.tensor_tensor(crow[:, w], st[:, :, :, w], convT[:, :, 24 + w:25 + w].to_broadcast([P, 12, NS]), ALU.mult).then_inc(*dv.done())
            for w in range(CW - 1):
                v.wait_ge(*dv.last())
                nc.vector.tensor_tensor(y, y, crow[:, w], ALU.add).then_inc(*dv.done("conv"))
            v.wait_ge(*pe.at("new_rows"))
            nc.vector.tensor_copy(work[0:11, A["oT"]:A["oT"] + CONV].rearrange("p (a b) -> p a b", a=3),
                                  ps[0:11, 5:8, :]).then_inc(*dv.done("conv_rest"))
            s5_tables_dve(v)

        def pc(v, i):
            return v.unsqueeze(2).to_broadcast([P, H, P])

        def banks(b, n=1):
            return ps[:, b:b + n, :].rearrange("p a b -> p (a b)")

        def bank4(b):
            return ps[:, b, :].rearrange("p (h n) -> p h n", h=H)

        def flat(v):
            return v.rearrange("p a b -> p (a b)")

        def gdn_pe(t):
            t.wait_ge(*ac.at("sq_cv"))
            for h in range(8):
                last = nc.tensor.matmul(ps[0:8, 0, 0:T], head_col[:, h], sq[:, h], start=h == 0, stop=h == 7)
            last.then_inc(*pe.done("ss"))
            t.wait_ge(*ac.at("rn"))
            t.wait_ge(*ac.at("proj31"))
            for h in range(8):
                nc.tensor.matmul(ps[:, h, 0:T], row_of(h, 8), R[0:8, RA], start=True, stop=True).then_inc(*pe.done(f"rn{h}"))
            t.wait_ge(*dv.at("qk_norm"))
            for i in range(TT):
                for h in range(H):
                    nc.tensor.transpose(bank4(i)[:, h], cv[:, 4 + h, i * P:(i + 1) * P], ident)
                for h in range(H):
                    last = nc.tensor.transpose(bank4(2 + i)[:, h], cv[:, 8 + h, i * P:(i + 1) * P], ident)
                last.then_inc(*pe.done(f"kv{i}"))
            for i in range(TT):
                for h in range(H):
                    k = cv[:, 4 + h, i * P:(i + 1) * P]
                    last = nc.tensor.matmul(bank4(4 + i)[:, h], k, k, start=True, stop=True)
            last.then_inc(*pe.done("kk"))
            for h in range(H):
                last = nc.tensor.matmul(ps[:, 6 + h // 2, (h % 2) * SEQ:(h % 2 + 1) * SEQ], row_of(h), R[0:H, RT_, 0:SEQ],
                                        start=True, stop=True)
            last.then_inc(*pe.done("G_all"))
            t.wait_ge(*dv.at("kv_tok"))
            for i in range(TT):
                for h in range(H):
                    last = nc.tensor.matmul(bank4(i)[:, h], cv[:, 4 + h, i * P:(i + 1) * P], cv[:, h, i * P:(i + 1) * P],
                                            start=True, stop=True)
            for h in range(H):
                for i in range(TT):
                    last = nc.tensor.matmul(bank4(2 + i)[:, h], row_of(h), R[0:H, RB_, i * P:(i + 1) * P], start=True, stop=True)
            last.then_inc(*pe.done("qk"))
            t.wait_ge(sem("states_in"), 16 * 2 * H)
            t.wait_ge(*dv.at("decay_in"))
            t.wait_ge(*ac.at("qdec"))
            t.wait_ge(*dv.at("kq"))
            for p in range(HS):
                nc.tensor.matmul(ps[:, 7, 2 * p:2 * p + 2], Sst[:, p], kq[:, :, p], start=True, stop=True)
            nc.tensor.matmul(ps[:, 7, 64:64 + HS], ones, small[:, 0], start=True, stop=True).then_inc(*pe.done("kS"))
            nc.tensor.transpose(ps[0:HS, 7, P:2 * P], kq[:, 0], ident).then_inc(*pe.done("krow"))
            for b in range(7):
                for i in range(TT):
                    if b == 0:
                        t.wait_ge(*po.at("tinit"))
                        t.wait_ge(*dv.at("attnT"))
                    else:
                        t.wait_ge(*dv.at(f"tinv{b - 1}.{i}"))
                    t.wait_ge(*po.at(f"level{b}"))
                    for h in range(H):
                        c = 4 * i + h
                        last = nc.tensor.matmul(bank4(i)[:, h], at_lev[b % 2][:, c], tinv[:, c], start=True, stop=True)
                    last.then_inc(*pe.done(f"z{b}.{i}"))
                for i in range(TT):
                    t.wait_ge(*ac.at(f"z{b}.{i}"))
                    if b > 0:
                        t.wait_ge(*dv.at(f"tinvT{b - 1}.{i}"))
                    if b < 6:
                        for h in range(H):
                            c = 4 * i + h
                            last = nc.tensor.matmul(bank4(2 + i)[:, h], tinvT[:, c], zz[:, c], start=True, stop=True)
                        last.then_inc(*pe.done(f"tz{b}.{i}"))
                    for h in range(H):
                        c = 4 * i + h
                        last = nc.tensor.matmul(bank4(4 + i)[:, h], zz[:, c], tinvT[:, c], start=True, stop=True)
                    last.then_inc(*pe.done(f"zt{b}.{i}"))
                if b == 0:
                    t.wait_ge(*dv.at("krow0"))
                    nc.tensor.transpose(ps[0:HS, 7, 2 * P:3 * P], small[:, 3], ident).then_inc(*pe.done("vrow"))
                if b >= 1:
                    for g in range(2 * b - 2, min(2 * b, 8)):
                        t.wait_ge(*po.at(f"vblkA{g}"))
                        t.wait_ge(*dv.at("krowA"))
                        if g >= 2:
                            t.wait_ge(*dv.at(f"newS{g - 2}"))
                        nc.tensor.matmul(banks(6 + g % 2), krow[0:HS, 0], flat(vblk[g % 2][0:HS]), start=True, stop=True).then_inc(*pe.done(f"outerA{g}"))
            for i in range(TT):
                t.wait_ge(*dv.at(f"tinvT6.{i}"))
            for h in range(H):
                last = nc.tensor.matmul(bank4(0)[:, h], tinvT[:, h], vb[:, h], start=True, stop=True)
            last.then_inc(*pe.done("v0"))
            for h in range(H):
                last = nc.tensor.matmul(bank4(1)[:, h], kbg[:, 4 + h], tinvT[:, 4 + h], start=True, stop=True)
            last.then_inc(*pe.done("wT"))
            t.wait_ge(*ac.at("v0"))
            for h in range(H):
                last = nc.tensor.matmul(bank4(2)[:, h], ktail[:, h], vnew[:, h], start=True, stop=True)
            last.then_inc(*pe.done("s1"))
            for h in range(H):
                last = nc.tensor.matmul(bank4(3)[:, h], vnew[:, h], attnT[:, h], start=True, stop=True)
            last.then_inc(*pe.done("o0"))
            t.wait_ge(*dv.at("s1"))
            t.wait_ge(*ac.at("wT"))
            for h in range(H):
                nc.tensor.matmul(bank4(4)[:, h], tinvT[:, 4 + h], vb[:, 4 + h], start=True, stop=False)
                last = nc.tensor.matmul(bank4(4)[:, h], negwT[:, h], s1[:, h], start=False, stop=True)
            last.then_inc(*pe.done("v1"))
            t.wait_ge(*ac.at("v1"))
            for h in range(H):
                nc.tensor.matmul(bank4(5)[:, h], vnew[:, h], attnT[:, 4 + h], start=True, stop=False)
                last = nc.tensor.matmul(bank4(5)[:, h], s1[:, h], qdec[:, h], start=False, stop=True)
            last.then_inc(*pe.done("o1"))
            t.wait_ge(*dv.at("newS7"))
            for h in range(H):
                last = nc.tensor.matmul(bank4(6)[:, h], ktail[:, 4 + h], vnew[:, h], start=True, stop=True)
            last.then_inc(*pe.done("s2"))

        at_lev = [at_l, dec]

        def gdn_act(a):
            a.wait_ge(*pe.at("ss"))
            nc.scalar.activation(R[0:8, RA], ps[0:8, 0, 0:T], ACT.Ln, bias=eps_rms[0:8]).then_inc(*ac.done())
            a.wait_ge(*ac.last())
            nc.scalar.activation(R[0:8, RA], R[0:8, RA], ACT.Exp, scale=-0.5).then_inc(*ac.done("rn"))
            a.wait_ge(*dv.at("decay_in"))
            nc.scalar.activation(flat(dec), flat(dec), ACT.Exp).then_inc(*ac.done("decay"))
            g_all = banks(6, 2).rearrange("p (h n) -> p h n", h=H)
            nc.scalar.activation(qdec, g_all[:, :, P:SEQ], ACT.Exp).then_inc(*ac.done())
            nc.scalar.activation(cd, g_all[:, :, SEQ - 1:SEQ].rearrange("p h o -> p (h o)"), ACT.Exp).then_inc(*ac.done("qdec"))
            for b in range(7):
                for i in range(TT):
                    a.wait_ge(*pe.at(f"z{b}.{i}"))
                    if b > 0:
                        a.wait_ge(*pe.at(f"zt{b - 1}.{i}"))
                    nc.scalar.copy(flat(zz[:, 4 * i:4 * i + 4]), banks(i)).then_inc(*ac.done(f"z{b}.{i}"))
            a.wait_ge(*pe.at("v0"))
            nc.scalar.copy(flat(vnew), banks(0)).then_inc(*ac.done("v0"))
            a.wait_ge(*pe.at("wT"))
            nc.scalar.mul(flat(negwT), banks(1), -1.0).then_inc(*ac.done("wT"))
            a.wait_ge(*pe.at("o0"))
            a.wait_ge(sem("stores_conv"), 32)
            nc.scalar.copy(oT[:, 0:4, 0:P], bank4(3)).then_inc(*ac.done())
            a.wait_ge(*pe.at("v1"))
            nc.scalar.copy(flat(vnew), banks(4)).then_inc(*ac.done("v1"))
            a.wait_ge(*pe.at("o1"))
            nc.scalar.copy(oT[:, 0:4, P:SEQ], bank4(5)).then_inc(*ac.done("oA"))

        def hs(v):
            return v.rearrange("p (h b) -> p h b", h=H)

        def gdn_dve(v):
            for h in range(8):
                v.wait_ge(*pe.at(f"rn{h}"))
                nc.vector.scalar_tensor_tensor(cv[:, h], cv[:, h], QSCALE if h < H else 1.0, ps[:, h, 0:T], ALU.mult, ALU.mult).then_inc(*dv.done("qk_norm"))
            v.wait_ge(*dv.last())
            nc.vector.tensor_copy(hs(kq[:, 0]), cv[:, 4:8, SEQ:]).then_inc(*dv.done())
            nc.vector.tensor_copy(hs(kq[:, 1]), cv[:, 0:4, SEQ:]).then_inc(*dv.done())
            nc.vector.tensor_tensor(hs(small[:, 0]), cv[:, 0:4, SEQ:], cv[:, 4:8, SEQ:], ALU.mult).then_inc(*dv.done("kq"))
            for i in range(TT):
                v.wait_ge(*pe.at(f"kv{i}"))
                for dst, src, col in ((kbg, i, BETA_EG), (ktail, i, TAIL_A), (vb, 2 + i, BETA)):
                    nc.vector.tensor_tensor(dst[:, 4 * i:4 * i + 4], bank4(src), pc(cols[:, col, i], i), ALU.mult).then_inc(*dv.done("kv_tok"))
            v.wait_ge(*pe.at("G_all"))
            for i in range(TT):
                for h in range(H):
                    at = (h % 2) * SEQ + i * P
                    nc.vector.tensor_scalar(dec[:, 4 * i + h], ps[:, 6 + h // 2, at:at + P], cols[:, NEG_G, i, h:h + 1], 0.0,
                                            ALU.add, ALU.min).then_inc(*dv.done("decay_in"))
            v.wait_ge(*ac.at("decay"))
            nc.vector.tensor_tensor(dec, dec, upper.unsqueeze(1).to_broadcast([P, 8, P]), ALU.mult).then_inc(*dv.done())
            v.wait_ge(*dv.last())
            v.wait_ge(*pe.at("kk"))
            nc.vector.tensor_tensor(flat(at_f), banks(4, 2), flat(dec), ALU.mult).then_inc(*dv.done())
            v.wait_ge(*dv.last())
            v.wait_ge(*pe.at("qk"))
            nc.vector.tensor_tensor(flat(at_f), flat(at_f), banks(2, 2), ALU.mult).then_inc(*dv.done("at_f"))
            nc.vector.tensor_tensor(flat(attnT), banks(0, 2), flat(dec), ALU.mult).then_inc(*dv.done("attnT"))
            v.wait_ge(*ac.at("qdec"))
            nc.vector.tensor_tensor(qdec, qdec, cv[:, 0:4, P:SEQ], ALU.mult).then_inc(*dv.done())
            v.wait_ge(*pe.at("krow"))
            kS = ps[:, 7, 0:64].rearrange("p (h b two) -> p h b two", h=H, two=2)
            nc.vector.tensor_tensor(hs(small[:, 1]), kS[:, :, :, 0], sb[:, :, EG], ALU.mult).then_inc(*dv.done())
            nc.vector.tensor_tensor(hs(small[:, 4]), kS[:, :, :, 1], sb[:, :, EG], ALU.mult).then_inc(*dv.done())
            v.wait_ge(*dv.last())
            nc.vector.tensor_tensor(hs(small[:, 2]), cv[:, 8:12, SEQ:], hs(small[:, 1]), ALU.subtract).then_inc(*dv.done())
            v.wait_ge(*dv.last())
            nc.vector.tensor_tensor(hs(small[:, 3]), hs(small[:, 2]), sb[:, :, BT], ALU.mult).then_inc(*dv.done("vS"))
            v.wait_ge(*dv.last())
            nc.vector.tensor_tensor(small[:, 5], ps[:, 7, 64:64 + HS], small[:, 3], ALU.mult).then_inc(*dv.done())
            v.wait_ge(*dv.last())
            v.wait_ge(sem("stores_conv"), 32)
            nc.vector.tensor_tensor(oT[:, 0:4, SEQ:], hs(small[:, 4]), hs(small[:, 5]), ALU.add).then_inc(*dv.done())
            v.wait_ge(*pe.at("krow"))
            nc.vector.tensor_copy(krow[0:HS, 0], ps[0:HS, 7, P:2 * P]).then_inc(*dv.done("krow0"))
            for b in range(7):
                for i in range(TT):
                    mine = slice(4 * i, 4 * i + 4)
                    if b < 6:
                        v.wait_ge(*pe.at(f"tz{b}.{i}"))
                        nc.vector.tensor_tensor(flat(tinv[:, mine]), flat(tinv[:, mine]), banks(2 + i), ALU.subtract).then_inc(*dv.done(f"tinv{b}.{i}"))
                    v.wait_ge(*pe.at(f"zt{b}.{i}"))
                    nc.vector.tensor_tensor(flat(tinvT[:, mine]), flat(tinvT[:, mine]), banks(4 + i), ALU.subtract).then_inc(*dv.done(f"tinvT{b}.{i}"))
                if b == 0:
                    v.wait_ge(*pe.at("vrow"))
                    nc.vector.tensor_copy(krow[0:HS, 1], ps[0:HS, 7, 2 * P:3 * P]).then_inc(*dv.done("krowA"))
                if b >= 1:
                    for g in range(2 * b - 2, min(2 * b, 8)):
                        v.wait_ge(*pe.at(f"outerA{g}"))
                        v.wait_ge(*po.at("scaleS"))
                        part = flat(Sst[:, 4 * g:4 * g + 4])
                        nc.vector.tensor_tensor(part, part, banks(6 + g % 2), ALU.add).then_inc(*dv.done(f"newS{g}"))
            v.wait_ge(*pe.at("s1"))
            nc.vector.tensor_copy(flat(s1), banks(2)).then_inc(*dv.done("s1"))
            v.wait_ge(*pe.at("s2"))
            for h in range(H):
                nc.vector.scalar_tensor_tensor(s1[:, h], s1[:, h], cd[:, h:h + 1], bank4(6)[:, h], ALU.mult, ALU.add).then_inc(*dv.done("s_final"))

        def outer_blocks(pool, row, steps, groups=range(8)):
            for g in groups:
                if g >= 2:
                    pool.wait_ge(*pe.at(f"outer{steps}{g - 2}"))
                elif steps == "B":
                    pool.wait_ge(*pe.at("outerA7"))
                nc.gpsimd.tensor_tensor(vblk[g % 2][0:HS], krow[0:HS, row].unsqueeze(1).to_broadcast([HS, 4, P]),
                                        ident[0:HS, 4 * g:4 * g + 4].unsqueeze(2).to_broadcast([HS, 4, P]),
                                        ALU.mult).then_inc(*po.done(f"vblk{steps}{g}"))

        def gdn_pool(pool):
            pool.wait_ge(*pe.at("proj31"))
            for dst in (tinv, tinvT):
                nc.gpsimd.tensor_copy(dst, ident.unsqueeze(1).to_broadcast([P, 8, P])).then_inc(*po.done("tinit"))
            for b in range(7):
                pool.wait_ge(*dv.at("attnT"))
                pool.wait_ge(*dv.at("levels"))
                if b >= 2:
                    pool.wait_ge(*pe.at(f"z{b - 2}.1"))
                nc.gpsimd.tensor_tensor(at_lev[b % 2], at_f, level[:, b].unsqueeze(1).to_broadcast([P, 8, P]),
                                        ALU.mult).then_inc(*po.done(f"level{b}"))
                if b == 1:
                    pool.wait_ge(*pe.at("krow"))
                    nc.gpsimd.tensor_tensor(Sst.rearrange("p (h b) v -> p h b v", h=H), Sst.rearrange("p (h b) v -> p h b v", h=H),
                                            sb[:, :, EG].unsqueeze(3).to_broadcast([P, H, NS, P]), ALU.mult).then_inc(*po.done("scaleS"))
                if b == 2:
                    nc.gpsimd.tensor_tensor(Cst.rearrange("p (h b) v -> p h b v", h=H), Cst.rearrange("p (h b) v -> p h b v", h=H),
                                            sb[:, :, FP].unsqueeze(3).to_broadcast([P, H, NS, P]), ALU.mult).then_inc(*po.done("scaleC"))
                if 2 <= b <= 5:
                    if b == 2:
                        pool.wait_ge(*dv.at("krowA"))
                    outer_blocks(pool, 1, "A", range(2 * b - 4, 2 * b - 2))

        def ml_pe(t):
            t.wait_ge(*dv.at("s_final"))
            t.wait_ge(*ac.at("oA"))
            for h in range(H):
                last = nc.tensor.matmul(ps[:, h // 2, (h % 2) * SEQ:(h % 2 + 1) * SEQ], row_of(h), R[0:H, RFM, 0:SEQ],
                                        start=True, stop=True)
            last.then_inc(*pe.done("FM_all"))
            for i in range(TT):
                for h in range(H):
                    nc.tensor.transpose(bank4(2)[:, h], pj[:, KB + h, i * P:(i + 1) * P], ident)
                for h in range(H):
                    last = nc.tensor.transpose(bank4(3)[:, h], pj[:, VB + h, i * P:(i + 1) * P], ident)
                last.then_inc(*pe.done(f"kvB{i}"))
                t.wait_ge(*dv.at(f"kwk{i}"))
                t.wait_ge(*ac.at(f"vm{i}"))
            for h in range(H):
                b = 4 + h
                k, q = pj[:, KB + h], pj[:, QB + h]
                nc.tensor.matmul(ps[:, b, 0:SEQ], k[:, 0:P], q[:, 0:SEQ], start=True, stop=True)
                last = nc.tensor.matmul(ps[:, b, SEQ:384], k[:, P:SEQ], q[:, P:SEQ], start=True, stop=True)
                last.then_inc(*pe.done(f"qkB{h}"))
            t.wait_ge(*dv.at("ik"))
            nc.tensor.transpose(ps[0:HS, 2, 0:P], small[:, 6], ident)
            nc.tensor.transpose(ps[0:HS, 2, P:2 * P], small[:, 7], ident)
            nc.tensor.transpose(ps[0:HS, 2, 2 * P:3 * P], small[:, 8], ident).then_inc(*pe.done("rowsB"))
            nc.tensor.matmul(ps[:, 2, 384:384 + HS], ones, small[:, 9], start=True, stop=True).then_inc(*pe.done("denS"))
            for h in range(H):
                for i in range(TT):
                    last = nc.tensor.matmul(bank4(3)[:, h], kwk[:, 4 * i + h], vm[:, 4 * i + h], start=i == 0, stop=i == TT - 1)
            last.then_inc(*pe.done("C"))
            t.wait_ge(*dv.at("wexp_in"))
            for h in range(H):
                for i in range(TT):
                    last = nc.tensor.matmul(ps[0:H, 0, 0:P], head_col[:, h, 0:H], kwk[:, 4 * i + h], start=(h, i) == (0, 0),
                                            stop=(h, i) == (H - 1, TT - 1))
            last.then_inc(*pe.done("n"))
            for h in range(H):
                t.wait_ge(*dv.at(f"wq{h}"))
                o = ps[:, 4 + h, 0:SEQ]
                nc.tensor.matmul(o, vm[:, h], wq[:, h, 0:SEQ], start=True, stop=False)
                nc.tensor.matmul(o[:, P:SEQ], vm[:, 4 + h], wq[:, h, SEQ:384], start=False, stop=True)
                den = ps[0:H, 1, 0:SEQ]
                nc.tensor.matmul(den, head_col[:, h, 0:H], wq[:, h, 0:SEQ], start=h == 0, stop=False)
                last = nc.tensor.matmul(den[:, P:SEQ], head_col[:, h, 0:H], wq[:, h, SEQ:384], start=False, stop=h == H - 1)
            last.then_inc(*pe.done("numden"))
            for g in range(8):
                t.wait_ge(*po.at(f"vblkB{g}"))
                if g == 0:
                    t.wait_ge(*dv.at("rowsB"))
                    t.wait_ge(*dv.at("C_out"))
                if g >= 2:
                    t.wait_ge(*dv.at(f"newC{g - 2}"))
                nc.tensor.matmul(banks(2 + g % 2), krow[0:HS, 2], flat(vblk[g % 2][0:HS]), start=True, stop=True).then_inc(*pe.done(f"outerB{g}"))
            t.wait_ge(*dv.at("newC7"))
            for p in range(HS):
                last = nc.tensor.matmul(ps[:, 2, p:p + 1], Cst[:, p], small[:, 10, p:p + 1], start=True, stop=True)
            last.then_inc(*pe.done("Cq"))
            t.wait_ge(*dv.at("rden"))
            t.wait_ge(*ac.at("numB"))
            for h in range(H):
                last = nc.tensor.matmul(ps[:, 4 + h, 0:SEQ], row_of(h), R[0:H, RKT, 0:SEQ], start=True, stop=True)
            last.then_inc(*pe.done("rden_all"))
            t.wait_ge(*ac.at("sq_o"))
            for h in range(8):
                last = nc.tensor.matmul(ps[0:8, 0, 0:T], head_col[:, h], sq[:, h], start=h == 0, stop=h == 7)
            last.then_inc(*pe.done("ss_o"))
            t.wait_ge(*ac.at("rn_o"))
            for h in range(8):
                nc.tensor.matmul(ps[:, h, 0:T], row_of(h, 8), R[0:8, RA], start=True, stop=True).then_inc(*pe.done(f"rno{h}"))
            t.wait_ge(sem("w_out"), 16)
            t.wait_ge(*dv.at("merged"))
            for i in range(TT):
                for k in range(8):
                    for n in range(2):
                        last = nc.tensor.matmul(ps[0:tok(i), 2 * i + n, :], oT[:, k, i * P:i * P + tok(i)], wout[:, k, n * 512:(n + 1) * 512],
                                                start=k == 0, stop=k == 7)
                last.then_inc(*pe.done(f"mixAB{i}"))
            for k in range(8):
                for n in range(2):
                    last = nc.tensor.matmul(ps[64 * n:64 * n + NS, 4, :], oT[:, k, SEQ:], wout[:, k, n * 512:(n + 1) * 512],
                                            start=k == 0, stop=k == 7)
            last.then_inc(*pe.done("mixAB2"))

        def ml_act(a):
            for i in range(TT):
                a.wait_ge(*pe.at(f"kvB{i}"))
                nc.scalar.copy(vm[:, 4 * i:4 * i + 4], bank4(3)).then_inc(*ac.done(f"vm{i}"))
            a.wait_ge(*dv.at("wexp_in"))
            nc.scalar.activation(flat(wexp), flat(wexp), ACT.Exp).then_inc(*ac.done("wexp"))
            a.wait_ge(*pe.at("numden"))
            nc.scalar.copy(oT[:, 4:8, 0:SEQ], ps[:, 4:8, 0:SEQ]).then_inc(*ac.done())
            nc.scalar.activation(R[0:H, RKT, 0:SEQ], ps[0:H, 1, 0:SEQ], ACT.Abs).then_inc(*ac.done("numB"))
            a.wait_ge(*dv.at("hB"))
            a.wait_ge(*ac.last())
            nc.scalar.activation(sq, oT, ACT.Square).then_inc(*ac.done("sq_o"))
            a.wait_ge(*pe.at("ss_o"))
            nc.scalar.activation(R[0:8, RA], ps[0:8, 0, 0:T], ACT.Ln, bias=eps_rms[0:8], scale=1.0 / DK).then_inc(*ac.done())
            a.wait_ge(*ac.last())
            nc.scalar.activation(R[0:8, RA], R[0:8, RA], ACT.Exp, scale=-0.5).then_inc(*ac.done("rn_o"))

        def ml_dve(v):
            for i in range(TT):
                v.wait_ge(*pe.at(f"kvB{i}"))
                nc.vector.tensor_tensor(kwk[:, 4 * i:4 * i + 4], bank4(2), pc(cols[:, TAIL_B, i], i), ALU.mult).then_inc(*dv.done(f"kwk{i}"))
            nc.vector.tensor_tensor(hs(small[:, 6]), pj[:, KB:KB + 4, SEQ:], sb[:, :, IP], ALU.mult).then_inc(*dv.done())
            nc.vector.tensor_copy(hs(small[:, 7]), pj[:, VB:VB + 4, SEQ:]).then_inc(*dv.done())
            nc.vector.tensor_copy(hs(small[:, 10]), pj[:, QB:QB + 4, SEQ:]).then_inc(*dv.done())
            nc.vector.tensor_tensor(hs(small[:, 8]), hs(paramsT[:, 2:34]), sb[:, :, FP], ALU.mult).then_inc(*dv.done())
            v.wait_ge(*dv.last())
            nc.vector.tensor_tensor(small[:, 8], small[:, 8], small[:, 6], ALU.add).then_inc(*dv.done())
            v.wait_ge(*dv.last())
            nc.vector.tensor_tensor(small[:, 9], small[:, 8], small[:, 10], ALU.mult).then_inc(*dv.done("ik"))
            v.wait_ge(*pe.at("FM_all"))
            for h in range(H):
                f = ps[:, h // 2, (h % 2) * SEQ:(h % 2 + 1) * SEQ]
                nc.vector.tensor_scalar(wexp[:, h, 0:SEQ], f, cols[:, I_F, 0, h:h + 1], 0.0, ALU.add, ALU.min).then_inc(*dv.done())
                nc.vector.tensor_scalar(wexp[:, h, SEQ:384], f[:, P:SEQ], cols[:, I_F, 1, h:h + 1], 0.0, ALU.add, ALU.min).then_inc(*dv.done("wexp_in"))
            v.wait_ge(*pe.at("denS"))
            for n, src in enumerate((0, 1)):
                nc.vector.tensor_copy(krow[0:HS, 2 + n], ps[0:HS, 2, src * P:(src + 1) * P]).then_inc(*dv.done())
            nc.vector.tensor_copy(nrow[0:HS], ps[0:HS, 2, 2 * P:3 * P]).then_inc(*dv.done())
            v.wait_ge(*pe.at("denS"))
            nc.vector.tensor_copy(small[:, 9], ps[:, 2, 384:384 + HS]).then_inc(*dv.done("rowsB"))
            v.wait_ge(*pe.at("C"))
            nc.vector.tensor_copy(flat(negwT), banks(3)).then_inc(*dv.done("C_out"))
            v.wait_ge(*ac.at("wexp"))
            for at in (0, SEQ):
                nc.vector.tensor_tensor(wexp[:, :, at:at + P], wexp[:, :, at:at + P], upper.unsqueeze(1).to_broadcast([P, H, P]), ALU.mult).then_inc(*dv.done())
            v.wait_ge(*dv.last())
            for h in range(H):
                v.wait_ge(*pe.at(f"qkB{h}"))
                nc.vector.tensor_tensor(wq[:, h], ps[:, 4 + h, 0:384], wexp[:, h], ALU.mult).then_inc(*dv.done(f"wq{h}"))
            v.wait_ge(*pe.at("n"))
            nc.vector.tensor_copy(qdec[0:H, 0], ps[0:H, 0, 0:P]).then_inc(*dv.done("n_out"))
            nc.vector.tensor_scalar(pj[:, OB:OB + 4], pj[:, OB:OB + 4], 0.5, 0.5, ALU.mult, ALU.add).then_inc(*dv.done("sig_o"))
            v.wait_ge(*ac.at("numB"))
            den = R[0:H, RKT, 0:SEQ]
            nc.vector.tensor_tensor(den, den, R[0:H, RG, 0:SEQ], ALU.max).then_inc(*dv.done())
            v.wait_ge(*dv.last())
            nc.vector.reciprocal(den, den).then_inc(*dv.done("rden"))
            for g in range(8):
                v.wait_ge(*pe.at(f"outerB{g}"))
                v.wait_ge(*po.at("scaleC"))
                part = flat(Cst[:, 4 * g:4 * g + 4])
                nc.vector.tensor_tensor(part, part, banks(2 + g % 2), ALU.add).then_inc(*dv.done(f"newC{g}"))
            s = small[:, 9]
            nc.vector.scalar_tensor_tensor(small[:, 8], s, -1.0, s, ALU.mult, ALU.max).then_inc(*dv.done())
            v.wait_ge(*dv.last())
            nc.vector.tensor_tensor(hs(small[:, 8]), hs(small[:, 8]), sb[:, :, EM], ALU.max).then_inc(*dv.done())
            v.wait_ge(*dv.last())
            nc.vector.reciprocal(small[:, 8], small[:, 8]).then_inc(*dv.done())
            v.wait_ge(*dv.last())
            v.wait_ge(*pe.at("Cq"))
            nc.vector.tensor_tensor(oT[:, 4:8, SEQ:], hs(ps[:, 2, 0:HS]), hs(small[:, 8]), ALU.mult).then_inc(*dv.done())
            v.wait_ge(*pe.at("rden_all"))
            nc.vector.tensor_tensor(oT[:, 4:8, 0:SEQ], oT[:, 4:8, 0:SEQ], ps[:, 4:8, 0:SEQ], ALU.mult).then_inc(*dv.done("hB"))
            for h in range(8):
                v.wait_ge(*pe.at(f"rno{h}"))
                nc.vector.scalar_tensor_tensor(oT[:, h], oT[:, h], paramsT[:, h // H:h // H + 1], ps[:, h, 0:T], ALU.mult, ALU.mult).then_inc(*dv.done())
            v.wait_ge(*dv.last())
            nc.vector.tensor_tensor(oT[:, 0:4], oT[:, 0:4], pj[:, Z_:Z_ + 4], ALU.mult).then_inc(*dv.done())
            nc.vector.tensor_tensor(oT[:, 4:8], oT[:, 4:8], pj[:, OB:OB + 4], ALU.mult).then_inc(*dv.done("merged"))

        def ml_pool(pool):
            pool.wait_ge(*dv.at("rowsB"))
            outer_blocks(pool, 3, "B")

        def ab_stores(sp):
            def store(dst, src):
                sp.dma_start(dst, src).then_inc(sem("stores"), 16)
            sp.wait_ge(*dv.at("conv_rest"))
            sp.dma_start(out["p_conv"][0, 0], work[0:3, A["oT"]:A["oT"] + CONV]).then_inc(sem("stores_conv"), 16)
            sp.dma_start(out["s_conv"][:, 0, 2], work[3:11, A["oT"]:A["oT"] + CONV]).then_inc(sem("stores_conv"), 16)
            sp.wait_ge(*dv.at("rows"))
            sp.dma_start(out["p_m"].rearrange("o a h -> h (o a)"), R[0:H, RM, SEQ - 1:SEQ]).then_inc(sem("stores"), 16)
            sp.dma_start(out["s_m"].rearrange("b o h -> h (o b)"), R[0:H, RM, SEQ:]).then_inc(sem("stores"), 16)
            sp.wait_ge(*dv.at("newS7"))
            for h in range(H):
                sp.dma_start(out["s_S"][:, 0, h].rearrange("b k v -> k b v"), Sst[:, h * NS:(h + 1) * NS]).then_inc(sem("stores"), 16)
            sp.wait_ge(*dv.at("s_final"))
            sp.dma_start(out["p_S"].rearrange("o a h k v -> k (o a h) v"), s1).then_inc(sem("stores_S"), 16)
            sp.wait_ge(*dv.at("C_out"))
            sp.dma_start(out["p_C"].rearrange("o a h k v -> k (o a h) v"), negwT).then_inc(sem("stores"), 16)
            sp.wait_ge(*dv.at("rowsB"))
            for h in range(H):
                sp.dma_start(out["s_n"][:, 0, h], nrow[h * NS:(h + 1) * NS]).then_inc(sem("stores"), 16)
            sp.wait_ge(*dv.at("n_out"))
            sp.dma_start(out["p_n"].rearrange("o a h k -> (o a h) k"), qdec[0:H, 0]).then_inc(sem("stores"), 16)
            sp.wait_ge(*dv.at("newC7"))
            for h in range(H):
                sp.dma_start(out["s_C"][:, 0, h].rearrange("b k v -> k b v"), Cst[:, h * NS:(h + 1) * NS]).then_inc(sem("stores_C"), 16)

        S5P = carve(ring, 8192, rows=2048, F=2048, tmp=2048, tmp_v=1024, cols=256, ldt=2)
        assert S5P["end"] <= 16384
        SR = view(ring, S5P["rows"], 15, P)[0:PT]
        (S_AR, S_AI, S_MAG, S_TH, S_K, S_SIN, S_COS, S_ABR, S_ABI, S_DEN, S_ZR, S_ZI, S_T1, S_T2, S_D) = range(15)
        ldt = view(ring, S5P["ldt"], 2)[0:PT]
        Fbuf = [view(ring, S5P[n], 2, 2, 2, SEQ) for n in ("F", "rows")]
        Ftmp_v = view(ring, S5P["tmp_v"], 2, 2, 2, P)
        Ftmp = view(ring, S5P["tmp"], 4, 2, 2, P)
        pcols = view(ring, S5P["cols"], 8, PT)
        F_dram = dram("rotations", (PT // 2, P, 2, 2, SEQ))
        cols_dram = dram("s5_cols", (P, 8 * PT))
        PI = 3.1415925
        ROUND = 1.5 * 2 ** 23
        TWO_PI_HI, TWO_PI_LO = 6.28125, 0.0019353071795864769

        def s5_param_loads(q):
            for i, name in ((S_AR, "s5_A_re"), (S_AI, "s5_A_im")):
                q.dma_start(SR[:, i], io[name].rearrange("o (t a) n -> (o t) (a n)", a=2)).then_inc(sem("s5_rows_in"), 16)
            q.dma_start(ldt, io["s5_log_dt"].rearrange("o (t a) -> (o t) a", a=2)).then_inc(sem("s5_rows_in"), 16)
            q.dma_start(SR[0:DC, S_D], io["s5_D"].rearrange("o (k p) -> (o k) p", p=P)).then_inc(sem("s5_rows_in"), 16)

        def s5_param_act0(a):
            a.wait_ge(sem("s5_rows_in"), 64)
            nc.scalar.activation(ldt, ldt, ACT.Exp).then_inc(*ac.done("s5_dt"))

        def s5_param_act1(a):
            a.wait_ge(*po.at("s5_x"))
            nc.scalar.activation(SR[:, S_MAG], SR[:, S_MAG], ACT.Exp).then_inc(*ac.done("s5_mag"))
            a.wait_ge(*po.at("s5_theta"))
            nc.scalar.activation(SR[:, S_SIN:S_COS + 1], SR[:, S_SIN:S_COS + 1], ACT.Sin).then_inc(*ac.done("s5_sin"))

        def s5_param_pool(pool):
            tt = lambda o, a, b, op, name=None: nc.gpsimd.tensor_tensor(SR[:, o], SR[:, a], SR[:, b], op).then_inc(*po.done(name))
            ts = lambda o, a, x, op0, y=None, op1=None, name=None: (nc.gpsimd.tensor_scalar(SR[:, o], SR[:, a], x, y, op0, op1) if op1 else
                                                                   nc.gpsimd.tensor_scalar(SR[:, o], SR[:, a], x, None, op0)).then_inc(*po.done(name))
            wait = lambda: pool.wait_ge(*po.last())
            pool.wait_ge(*ac.at("s5_dt"))
            half = lambda i: SR[:, i].rearrange("p (a n) -> p a n", a=2)
            dt = ldt.unsqueeze(2).to_broadcast([PT, 2, N5])
            nc.gpsimd.tensor_tensor(half(S_MAG), half(S_AR), dt, ALU.mult).then_inc(*po.done("s5_x"))
            nc.gpsimd.tensor_tensor(half(S_TH), half(S_AI), dt, ALU.mult).then_inc(*po.done())
            wait()
            ts(S_K, S_TH, 1.0 / 6.283185307179586, ALU.mult, ROUND, ALU.add)
            wait()
            ts(S_K, S_K, -ROUND, ALU.add)
            wait()
            ts(S_T1, S_K, -TWO_PI_HI, ALU.mult)
            wait()
            tt(S_TH, S_TH, S_T1, ALU.add)
            ts(S_T2, S_K, -TWO_PI_LO, ALU.mult)
            wait()
            tt(S_TH, S_TH, S_T2, ALU.add)
            wait()
            ts(S_SIN, S_TH, -PI, ALU.max, PI, ALU.min, name="s5_wrapped")
            pool.wait_ge(*dv.at("s5_abs"))
            ts(S_COS, S_COS, -1.0, ALU.mult, PI / 2, ALU.add, name="s5_theta")
            tt(S_T1, S_AR, S_AR, ALU.mult)
            tt(S_T2, S_AI, S_AI, ALU.mult)
            wait()
            tt(S_DEN, S_T1, S_T2, ALU.add, name="s5_den")
            pool.wait_ge(*ac.at("s5_sin"))
            tt(S_ABR, S_MAG, S_COS, ALU.mult)
            tt(S_ABI, S_MAG, S_SIN, ALU.mult)
            wait()
            ts(S_K, S_ABR, -1.0, ALU.add)
            wait()
            tt(S_T1, S_K, S_AR, ALU.mult)
            tt(S_T2, S_ABI, S_AI, ALU.mult)
            wait()
            tt(S_ZR, S_T1, S_T2, ALU.add)
            wait()
            tt(S_T1, S_ABI, S_AR, ALU.mult)
            tt(S_T2, S_K, S_AI, ALU.mult)
            wait()
            tt(S_ZI, S_T1, S_T2, ALU.subtract)
            pool.wait_ge(*dv.at("s5_rden"))
            wait()
            tt(S_ZR, S_ZR, S_DEN, ALU.mult)
            tt(S_ZI, S_ZI, S_DEN, ALU.mult, name="s5_rows")

        def s5_param_dve(v):
            v.wait_ge(*po.at("s5_wrapped"))
            nc.vector.scalar_tensor_tensor(SR[:, S_COS], SR[:, S_SIN], -1.0, SR[:, S_SIN], ALU.mult, ALU.max).then_inc(*dv.done("s5_abs"))
            v.wait_ge(*po.at("s5_den"))
            nc.vector.reciprocal(SR[:, S_DEN], SR[:, S_DEN]).then_inc(*dv.done("s5_rden"))

        def s5_param_pe(t):
            t.wait_ge(*po.at("s5_rows"))
            for i, r in enumerate((S_COS, S_SIN, S_MAG, S_ABR, S_ABI, S_ZR, S_ZI)):
                nc.tensor.transpose(ps[:, 7, i * PT:(i + 1) * PT], SR[:, r], ident[0:PT, 0:PT])
            nc.tensor.transpose(ps[:, 7, 7 * PT:7 * PT + DC], SR[0:DC, S_D], ident[0:DC, 0:DC]).then_inc(*pe.done("s5_cols"))

        def s5_cols_dve(v):
            v.wait_ge(*pe.at("s5_cols"))
            flat_cols = pcols.rearrange("p a b -> p (a b)")
            nc.vector.memset(flat_cols[:, 7 * PT:], 0.0).then_inc(*dv.done())
            v.wait_ge(*dv.last())
            nc.vector.tensor_copy(flat_cols[:, 0:7 * PT + DC], ps[:, 7, 0:7 * PT + DC]).then_inc(*dv.done("s5_cols"))

        BATCHES, POOL_BATCHES, TABLE_STEPS = PT // 4, 5, 2 + 6 * 8

        def table_batch(eng, tensor_tensor, name, buf, tmp, b, base, stored):
            tab = sem(f"table_steps_{name}")
            if stored is not None:
                eng.wait_ge(sem(f"tables_out_{name}"), stored)
            for w in range(2):
                tensor_tensor(buf[:, :, w, :, 0:1], pcols[:, w, bass.ds(4 * b, 4)].rearrange("p (a b o) -> p a b o", a=2, o=1),
                              ones[:, 0:4].rearrange("p (a b o) -> p a b o", a=2, o=1), ALU.mult).then_inc(tab, 1)
            for k in range(8):
                n = 2 ** k
                re, im = buf[:, :, 0, :, 0:n], buf[:, :, 1, :, 0:n]
                cr, ci = (buf[:, :, w, :, n - 1:n].to_broadcast([P, 2, 2, n]) for w in range(2))
                pairs = ((re, cr), (im, ci)), ((re, ci), (im, cr))
                slots = len(tmp)
                at = base + 2 + 6 * k
                eng.wait_ge(tab, at)
                for w, two in enumerate(pairs):
                    t = tmp[2 * w:2 * w + 2] if slots == 4 else tmp
                    if slots == 2 and w == 1:
                        eng.wait_ge(tab, at + 3)
                    for i, (x, y) in enumerate(two):
                        tensor_tensor(t[i][:, :, :, 0:n], x, y, ALU.mult).then_inc(tab, 1)
                    if slots == 2:
                        eng.wait_ge(tab, at + 3 * w + 2)
                        tensor_tensor(buf[:, :, w, :, n:2 * n], t[0][:, :, :, 0:n], t[1][:, :, :, 0:n], (ALU.subtract, ALU.add)[w]).then_inc(tab, 1)
                if slots == 4:
                    eng.wait_ge(tab, at + 4)
                    for w in range(2):
                        tensor_tensor(buf[:, :, w, :, n:2 * n], tmp[2 * w][:, :, :, 0:n], tmp[2 * w + 1][:, :, :, 0:n], (ALU.subtract, ALU.add)[w]).then_inc(tab, 1)

        def s5_tables_pool(pool):
            pool.wait_ge(*dv.at("s5_cols"))
            tmp = [Ftmp[:, i] for i in range(4)]
            table_batch(pool, nc.gpsimd.tensor_tensor, "p", Fbuf[0], tmp, 0, 0, None)
            with pool.Fori(1, POOL_BATCHES) as b:
                table_batch(pool, nc.gpsimd.tensor_tensor, "p", Fbuf[0], tmp, b, TABLE_STEPS * b, 16 * b)

        def s5_tables_dve(v):
            v.wait_ge(*dv.at("s5_cols"))
            tmp = [Ftmp_v[:, i] for i in range(2)]
            table_batch(v, nc.vector.tensor_tensor, "v", Fbuf[1], tmp, POOL_BATCHES, 0, None)
            with v.Fori(1, BATCHES - POOL_BATCHES) as b:
                table_batch(v, nc.vector.tensor_tensor, "v", Fbuf[1], tmp, b + POOL_BATCHES, TABLE_STEPS * b, 16 * b)

        def s5_tables_store(q):
            def store(name, b):
                q.wait_ge(sem(f"table_steps_{name}"), TABLE_STEPS * b + TABLE_STEPS)
                at = 2 * b + (2 * POOL_BATCHES if name == "v" else 0)
                q.dma_start(F_dram.rearrange("j p w t n -> p j (w t n)")[:, bass.ds(at, 2)],
                            Fbuf["pv".index(name)].rearrange("p j w t n -> p j (w t n)")).then_inc(sem(f"tables_out_{name}"), 16)
            with q.Fori(0, POOL_BATCHES - 1) as b:
                store("p", b)
            for name, b in (("v", 0), ("v", 1), ("p", POOL_BATCHES - 1), ("v", 2)):
                store(name, b)

        def s5_cols_store(q):
            q.wait_ge(*dv.at("s5_cols"))
            q.dma_start(cols_dram, pcols.rearrange("p a b -> p (a b)")).then_inc(sem("cols_out"), 16)

        def s5_tables_stored(q):
            q.wait_ge(sem("cols_out"), 16)
            q.wait_ge(sem("tables_out_p"), 16 * POOL_BATCHES)
            q.wait_ge(sem("tables_out_v"), 16 * (BATCHES - POOL_BATCHES))

        M = carve(work, A["cv"] + 3 * D, mix=0, ybuf=3 * 2 * D, xg=2 * D, xgT=2 * DC * SLOT, sghid=2 * FF,
                  hidT=2 * 4 * SLOT, yo=2 * D, route=14 * 48, gidx=96, addr=12, icol=8, carry=1, cnt=2, stats=64)
        lnp_at = A["end"]
        assert M["end"] <= lnp_at and lnp_at + 2 * D <= WORK, (M["end"], lnp_at)
        xres = xtok
        lnp = view(work, lnp_at, 2, D)
        ybuf = view(work, M["ybuf"], 3, 2, D)
        xg = [view(work, M["xg"] + s * D, D) for s in range(2)]
        xgT = [view(work, M["xgT"] + s * DC * SLOT, DC, SLOT) for s in range(2)]
        sg = [view(work, M["sghid"] + s * FF, FF) for s in range(2)]
        hid = sg
        hidT = [view(work, M["hidT"] + s * 4 * SLOT, 4, SLOT) for s in range(2)]
        yo = [view(work, M["yo"] + s * D, D) for s in range(2)]
        FIX = DC * NE + NE + P + 32 + 12
        fix = ctx.enter_context(nc.sbuf_tensor("fix", [P, FIX + 96], F32))
        lst = view(fix, FIX, 96).bitcast(I32)[:, 0:LISTS + 2]
        gidx = view(work, M["gidx"], 96).bitcast(I32)[:, 0:LISTS + 2]
        addr = view(work, M["addr"], 2, 3).bitcast(I32)
        icol = view(work, M["icol"], 2, 2).bitcast(I32)
        cnt = view(work, M["cnt"], 2)
        carry = view(work, M["carry"], 1)[0:1]
        stats = view(work, M["stats"], 3, 2, 6)
        mv = view(work, M["stats"] + 36, 3, 2)
        rstd = view(work, M["stats"] + 42, 3, 2)
        comb = view(work, M["stats"] + 48, 2, 3)

        def rt(i, *shape):
            return view(work, M["route"] + 48 * i, *(shape or (3, NE)))

        router = view(fix, 0, DC, NE)
        router_b = view(fix, DC * NE, NE)
        before = view(fix, DC * NE + NE, P)
        o_ = DC * NE + NE + P
        rank16 = view(fix, o_, NE)
        iota16 = view(fix, o_ + NE, NE)
        value = view(fix, o_ + 2 * NE, 3, 2).bitcast(I32)
        valid = view(fix, o_ + 2 * NE + 6, 3)
        x_dram = [dram(f"x_rows{l}", (T, D)) for l in range(2)]
        y_dram = [dram(f"y_rows{l}", (2 * T, D)) for l in range(2)]
        list_dram = [dram(f"lists{l}", (SLOT, LISTS), I32) for l in range(2)]

        def moe_consts_pool(pool):
            nc.gpsimd.memset(rank16, 0.0).then_inc(*po.done())
            i16 = lst[:, 0:NE]
            nc.gpsimd.iota(i16, pattern=[[1, NE]], base=0, channel_multiplier=0).then_inc(*po.done())
            nc.gpsimd.iota(value, pattern=[[2 * P, 3], [1, 2]], base=0, channel_multiplier=2).then_inc(*po.done())
            nc.gpsimd.memset(valid, 1.0).then_inc(*po.done())
            pool.wait_ge(*po.last())
            nc.gpsimd.affine_select(out=valid[:, TT:TT + 1], in_=valid[:, TT:TT + 1], pattern=[[0, 1]], compare_op=ALU.is_ge,
                                    fill=0.0, base=NS - 1, channel_multiplier=-1).then_inc(*po.done())
            nc.gpsimd.tensor_copy(iota16, i16).then_inc(*po.done())
            nc.gpsimd.tensor_tensor(before, upper, ident, ALU.subtract).then_inc(*po.done())
            pool.wait_ge(*po.last())
            nc.gpsimd.tensor_scalar(rank16, iota16, -1.0, float(NE), ALU.mult, ALU.add).then_inc(*po.done())
            pool.wait_ge(*po.last())
            nc.gpsimd.memset(lst, NOWHERE).then_inc(*po.done("lists_empty"))

        def moe_consts_loads(q):
            q.dma_start(router, io["router_w"].rearrange("(k p) e -> p k e", p=P)).then_inc(sem("router_in"), 16)
            q.dma_start(router_b, io["router_b"].partition_broadcast(P)).then_inc(sem("router_in"), 16)
            q.wait_ge(*po.at("lists_empty"))
            for l in range(2):
                q.dma_start(list_dram[l], lst[0:SLOT, 0:LISTS]).then_inc(sem("lists_empty"), 16)

        def ln_load(q, name_g, name_b, layer, wait):
            if wait is not None:
                q.wait_ge(*wait)
            for i, n in enumerate((name_g, name_b)):
                q.dma_start(lnp[:, i], io[n][layer].partition_broadcast(P)).then_inc(sem("lnp_in"), 16)

        def ln_dve(v, tag, nth, add):
            for i in range(3):
                n = tok(i)
                add(i, n)
                v.wait_ge(*dv.last())
                for c in range(2):
                    nc.vector.bn_stats(stats[0:n, i, c], xres[0:n, i, c * 512:(c + 1) * 512]).then_inc(*dv.done())
                v.wait_ge(*dv.last())
                nc.vector.bn_aggr(mv[0:n, i], stats[0:n, i].rearrange("p a b -> p (a b)")).then_inc(*dv.done(f"{tag}mv{i}"))
            for i in range(3):
                n = tok(i)
                v.wait_ge(*ac.at(f"{tag}rstd{i}"))
                nc.vector.tensor_scalar(xres[0:n, i], xres[0:n, i], mv[0:n, i, 0:1], rstd[0:n, i, 0:1], ALU.subtract, ALU.mult).then_inc(*dv.done())
                v.wait_ge(*dv.last())
                v.wait_ge(sem("lnp_in"), 32 * nth)
                nc.vector.tensor_tensor(xres[0:n, i], xres[0:n, i], lnp[0:n, 0], ALU.mult).then_inc(*dv.done(f"{tag}g{i}"))

        def ln_act(a, tag):
            for i in range(3):
                n = tok(i)
                a.wait_ge(*dv.at(f"{tag}mv{i}"))
                nc.scalar.activation(rstd[0:n, i, 0:1], mv[0:n, i, 1:2], ACT.Ln, bias=eps_ln[0:n]).then_inc(*ac.done())
                a.wait_ge(*ac.last())
                nc.scalar.activation(rstd[0:n, i, 0:1], rstd[0:n, i, 0:1], ACT.Exp, scale=-0.5).then_inc(*ac.done(f"{tag}rstd{i}"))

        def ln_pool(pool, tag):
            for i in range(3):
                n = tok(i)
                pool.wait_ge(*dv.at(f"{tag}g{i}"))
                nc.gpsimd.tensor_tensor(xres[0:n, i], xres[0:n, i], lnp[0:n, 1], ALU.add).then_inc(*po.done(f"{tag}x{i}"))

        def xT_pe(t, tag, free):
            for f in free:
                t.wait_ge(*f)
            for i in range(3):
                t.wait_ge(*po.at(f"{tag}x{i}"))
            for k in range(DC):
                for i in range(3):
                    last = nc.tensor.transpose(ps[:, k, i * P:i * P + tok(i)], xres[0:tok(i), i, k * P:(k + 1) * P],
                                               ident[0:tok(i), 0:tok(i)])
                last.then_inc(*pe.done(f"{tag}xT{k}"))

        def xT_copy(eng, steps, copy, tag, first):
            for k in range(first, DC, 2):
                eng.wait_ge(*pe.at(f"{tag}xT{k}"))
                copy(xT[:, k], ps[:, k, 0:T]).then_inc(*steps.done(f"{tag}xT"))

        def route_pe(t, tag):
            t.wait_ge(*ac.at(f"{tag}xT"))
            t.wait_ge(*dv.at(f"{tag}xT"))
            t.wait_ge(sem("router_in"), 32)
            for i in range(3):
                for k in range(DC):
                    last = nc.tensor.matmul(ps[0:tok(i), 0, i * NE:(i + 1) * NE], xT[:, k, i * P:i * P + tok(i)], router[:, k],
                                            start=k == 0, stop=k == DC - 1)
            last.then_inc(*pe.done(f"{tag}logits"))
            t.wait_ge(*dv.at(f"{tag}mask"))
            mask = rt(9)
            for i in range(3):
                for j in range(i):
                    nc.tensor.matmul(ps[:, 1, i * NE:(i + 1) * NE], ones, mask[:, j], start=j == 0, stop=False)
                nc.tensor.matmul(ps[:, 1, i * NE:(i + 1) * NE], before, mask[:, i], start=i == 0, stop=True)
            for i in range(3):
                last = nc.tensor.matmul(ps[:, 1, 48:48 + NE], ones, mask[:, i], start=i == 0, stop=i == 2)
            last.then_inc(*pe.done(f"{tag}pos"))

        def route_act(a, tag):
            a.wait_ge(*dv.at(f"{tag}shifted"))
            nc.scalar.activation(rt(1), rt(1), ACT.Exp).then_inc(*ac.done(f"{tag}exp"))

        def route_dve(v, tag):
            bc = lambda a, n: a.unsqueeze(2).to_broadcast([P, a.shape[1], n])
            red = lambda o, x, op: nc.vector.tensor_reduce(o, x, AX, op)
            r3 = lambda i: rt(i, 48)[:, 0:3]
            logit, e, sel = rt(0), rt(1), rt(2)

            def first_max(dst, x, n, groups, tmp, small):
                m = rt(small, 48)[:, 0:groups]
                red(m, x, ALU.max).then_inc(*dv.done())
                v.wait_ge(*dv.last())
                nc.vector.tensor_tensor(tmp, x, bc(m, n), ALU.is_equal).then_inc(*dv.done())
                v.wait_ge(*dv.last())
                nc.vector.tensor_tensor(tmp, tmp, rank16[:, NE - n:].unsqueeze(1).to_broadcast([P, groups, n]), ALU.mult).then_inc(*dv.done())
                v.wait_ge(*dv.last())
                red(m, tmp, ALU.max).then_inc(*dv.done())
                v.wait_ge(*dv.last())
                nc.vector.tensor_tensor(dst, tmp, bc(m, n), ALU.is_equal).then_inc(*dv.done())
                v.wait_ge(*dv.last())

            nc.vector.memset(logit, 0.0).then_inc(*dv.done())
            v.wait_ge(*dv.last())
            v.wait_ge(*pe.at(f"{tag}logits"))
            nc.vector.tensor_copy(logit[:, 0:TT], ps[:, 0, 0:TT * NE].rearrange("p (a b) -> p a b", a=TT)).then_inc(*dv.done())
            nc.vector.tensor_copy(logit[0:NS, TT], ps[0:NS, 0, TT * NE:3 * NE]).then_inc(*dv.done())
            v.wait_ge(*dv.last())
            red(r3(3), logit, ALU.max).then_inc(*dv.done())
            v.wait_ge(*dv.last())
            nc.vector.tensor_tensor(e, logit, bc(r3(3), NE), ALU.subtract).then_inc(*dv.done(f"{tag}shifted"))
            v.wait_ge(*ac.at(f"{tag}exp"))
            red(r3(3), e, ALU.add).then_inc(*dv.done())
            v.wait_ge(*dv.last())
            nc.vector.reciprocal(r3(3), r3(3)).then_inc(*dv.done())
            v.wait_ge(*dv.last())
            nc.vector.tensor_tensor(e, e, bc(r3(3), NE), ALU.mult).then_inc(*dv.done())
            v.wait_ge(*dv.last())
            nc.vector.tensor_tensor(sel, e, router_b.unsqueeze(1).to_broadcast([P, 3, NE]), ALU.add).then_inc(*dv.done())
            v.wait_ge(*dv.last())
            g4 = sel.rearrange("p a (g k) -> p (a g) k", k=EPG)
            part = lambda i: rt(4, 4, 12)[:, i]
            for i, (a, b, op) in enumerate(((0, 1, ALU.max), (0, 1, ALU.min), (2, 3, ALU.max), (2, 3, ALU.min))):
                nc.vector.tensor_tensor(part(i), g4[:, :, a], g4[:, :, b], op).then_inc(*dv.done())
            v.wait_ge(*dv.last())
            p2 = lambda i: rt(5, 4, 12)[:, i]
            nc.vector.tensor_tensor(p2(0), part(0), part(2), ALU.max).then_inc(*dv.done())
            nc.vector.tensor_tensor(p2(1), part(0), part(2), ALU.min).then_inc(*dv.done())
            nc.vector.tensor_tensor(p2(2), part(1), part(3), ALU.max).then_inc(*dv.done())
            v.wait_ge(*dv.last())
            nc.vector.tensor_tensor(p2(1), p2(1), p2(2), ALU.max).then_inc(*dv.done())
            v.wait_ge(*dv.last())
            nc.vector.tensor_tensor(p2(3), p2(0), p2(1), ALU.add).then_inc(*dv.done())
            v.wait_ge(*dv.last())
            g_hot = rt(4, 48)[:, 0:12]
            first_max(g_hot.rearrange("p (a g) -> p a g", g=NG), p2(3).rearrange("p (a g) -> p a g", g=NG), NG, 3,
                      rt(6, 48)[:, 0:12].rearrange("p (a g) -> p a g", g=NG), 3)
            inside = rt(6, 12, EPG)
            nc.vector.tensor_copy(inside, g_hot.unsqueeze(2).to_broadcast([P, 12, EPG])).then_inc(*dv.done())
            v.wait_ge(*dv.last())
            nc.vector.tensor_tensor(sel, sel, rt(6), ALU.mult).then_inc(*dv.done())
            nc.vector.tensor_scalar(rt(6), rt(6), 1e30, -1e30, ALU.mult, ALU.add).then_inc(*dv.done())
            v.wait_ge(*dv.last())
            nc.vector.tensor_tensor(sel, sel, rt(6), ALU.add).then_inc(*dv.done())
            v.wait_ge(*dv.last())
            hot = [rt(7), rt(8)]
            first_max(hot[0], sel, NE, 3, rt(6), 3)
            nc.vector.scalar_tensor_tensor(rt(2, 48), rt(7, 48), -4e30, rt(2, 48), ALU.mult, ALU.add).then_inc(*dv.done())
            v.wait_ge(*dv.last())
            first_max(hot[1], sel, NE, 3, rt(6), 3)
            nc.vector.tensor_tensor(rt(9), hot[0], hot[1], ALU.add).then_inc(*dv.done())
            v.wait_ge(*dv.last())
            nc.vector.tensor_tensor(rt(9), rt(9), bc(valid, NE), ALU.mult).then_inc(*dv.done(f"{tag}mask"))
            for j in range(2):
                nc.vector.tensor_tensor(rt(10 + j), hot[j], e, ALU.mult).then_inc(*dv.done())
            v.wait_ge(*dv.last())
            for j in range(2):
                red(comb[:, j], rt(10 + j), ALU.add).then_inc(*dv.done())
            v.wait_ge(*dv.last())
            nc.vector.tensor_tensor(r3(3), comb[:, 0], comb[:, 1], ALU.add).then_inc(*dv.done())
            v.wait_ge(*dv.last())
            nc.vector.reciprocal(r3(3), r3(3)).then_inc(*dv.done())
            v.wait_ge(*dv.last())
            nc.vector.tensor_tensor(comb, comb, r3(3).unsqueeze(1).to_broadcast([P, 2, 3]), ALU.mult).then_inc(*dv.done())
            v.wait_ge(*pe.at(f"{tag}pos"))
            pos = rt(6)
            nc.vector.tensor_copy(pos, ps[:, 1, 0:48].rearrange("p (a b) -> p a b", a=3)).then_inc(*dv.done())
            red(cnt[:, 0:1], ps[:, 1, 48:48 + NE], ALU.max).then_inc(*dv.done())
            v.wait_ge(*dv.last())
            nc.vector.tensor_copy(cnt[:, 1:2].bitcast(I32), cnt[:, 0:1]).then_inc(*dv.done(f"{tag}cnt"))
            for j in range(2):
                nc.vector.tensor_tensor(rt(10 + j), hot[j], pos, ALU.mult).then_inc(*dv.done())
                nc.vector.tensor_tensor(rt(12 + j), hot[j], iota16.unsqueeze(1).to_broadcast([P, 3, NE]), ALU.mult).then_inc(*dv.done())
            v.wait_ge(*dv.last())
            at = rt(3, 48)[:, 0:18].rearrange("p (a j i) -> p a j i", a=3, j=2)
            for j in range(2):
                red(at[:, 0, j], rt(10 + j), ALU.add).then_inc(*dv.done())
                red(at[:, 1, j], rt(12 + j), ALU.add).then_inc(*dv.done())
            v.wait_ge(*dv.last())
            nc.vector.scalar_tensor_tensor(at[:, 1], at[:, 0], float(LISTS), at[:, 1], ALU.mult, ALU.add).then_inc(*dv.done())
            for r in range(1, ROUNDS):
                nc.vector.tensor_scalar(at[:, 2], at[:, 0], float(SLOT * r), float(NE - SLOT * LISTS), ALU.is_ge, ALU.mult).then_inc(*dv.done())
                v.wait_ge(*dv.last())
                nc.vector.tensor_tensor(at[:, 1], at[:, 1], at[:, 2], ALU.add).then_inc(*dv.done())
                v.wait_ge(*dv.last())
            nc.vector.tensor_copy(addr, at[:, 1]).then_inc(*dv.done(f"{tag}addr"))

        def route_lists(v, tag):
            v.wait_ge(sem("lists_in"), 16 * (1 + int(tag[1]) // 2))
            nc.vector.tensor_single_scalar(gidx[0:SLOT], lst[0:SLOT], 1, ALU.logical_shift_right).then_inc(*dv.done(f"{tag}gidx"))

        def route_pool(pool, tag, l):
            pool.wait_ge(*dv.at(f"{tag}addr"))
            pool.wait_ge(sem("lists_empty"), 32)
            flat_list = list_dram[l].rearrange("s (n o) -> (s n) o", o=1)
            for i in range(3):
                for j in range(2):
                    pool.indirect_dma_start(flat_list, bass.IndirectOffsetOnAxis(ap=addr[0:tok(i), j, i:i + 1].bitcast(U32), axis=0),
                                            value[0:tok(i), i, j:j + 1], None,
                                            bounds_check=SLOT * LISTS - 1, oob_is_err=False).then_inc(sem(f"listed{l}"), 16)
            pool.wait_ge(sem(f"listed{l}"), 16 * 6)
            pool.dma_start(lst[0:SLOT, 0:LISTS], list_dram[l]).then_inc(sem("lists_in"), 16)

        def route_loads(q, tag, l):
            for i in range(3):
                q.wait_ge(*po.at(f"{tag}x{i}"))
                q.dma_start(x_dram[l][i * P:i * P + tok(i)], xres[0:tok(i), i]).then_inc(sem(f"x_rows{l}"), 16)

        def waits(eng, l):
            return lambda name, value: eng.wait_ge(sem(f"{name}{l}"), value)

        def expert_weights(q, l, k, e, u, s, first):
            w = waits(q, l)
            if not first:
                w("pe_moe", 4 * k - 6)
            for dst, name in ((gate_w[s], "moe_w_gate"), (up_w[s], "moe_w_up")):
                q.dma_start(dst, io[name][l].rearrange("e (k p) f -> p (e k) f", p=P)[:, bass.ds(e * DC, DC), :]).then_inc(sem(f"w_gu{s}_{l}"), 16)
            if not first:
                w("pe_moe", 4 * k - 4)
            q.dma_start(down_w[s], io["moe_w_down"][l].rearrange("e (k p) f -> p (e k) f", p=P)[:, bass.ds(e * 4, 4), :]).then_inc(sem(f"w_dn{s}_{l}"), 16)

        def expert_pe(t, l, k, u, s, first):
            w = waits(t, l)

            def to_features(bank, rows, chunks):
                for c in range(chunks):
                    op = nc.tensor.matmul if c == 0 else nc.tensor.transpose
                    last = op(bank[:, c * SLOT:(c + 1) * SLOT], rows[0:SLOT, c * P:(c + 1) * P], ident[0:SLOT, 0:SLOT],
                              **(dict(start=True, stop=True) if c == 0 else {}))
                last.then_inc(sem(f"pe_moe{l}"), 1)

            t.wait_ge(sem(f"xg{s}_{l}"), 16 * u + 16)
            to_features(ps[:, s], xg[s], DC)
            w("act_moe", 3 * k + 1)
            t.wait_ge(sem(f"w_gu{s}_{l}"), 32 * u + 32)
            if not first:
                w("dve_moe", 3 * k - 5)
            for c in range(DC):
                nc.tensor.matmul(ps[0:SLOT, 2 + s, :], xgT[s][:, c], gate_w[s][:, c], start=c == 0, stop=c == DC - 1)
                last = nc.tensor.matmul(ps[SLOT:P, 2 + s, :], xgT[s][:, c], up_w[s][:, c], start=c == 0, stop=c == DC - 1)
            last.then_inc(sem(f"pe_moe{l}"), 1)
            w("dve_moe", 3 * k + 1)
            to_features(ps[:, 4 + s], hid[s], 4)
            w("dve_moe", 3 * k + 2)
            t.wait_ge(sem(f"w_dn{s}_{l}"), 16 * u + 16)
            if not first:
                w("dve_moe", 3 * k - 3)
                w("act_moe", 3 * k - 3)
            for c in range(4):
                nc.tensor.matmul(ps[0:SLOT, 6 + s, :], hidT[s][:, c], down_w[s][:, c, 0:512], start=c == 0, stop=c == 3)
                last = nc.tensor.matmul(ps[SLOT:P, 6 + s, :], hidT[s][:, c], down_w[s][:, c, 512:D], start=c == 0, stop=c == 3)
            last.then_inc(sem(f"pe_moe{l}"), 1)

        def expert_act(a, l, k, u, s, first):
            w = waits(a, l)
            w("pe_moe", 4 * k + 1)
            nc.scalar.copy(xgT[s].rearrange("p a b -> p (a b)"), ps[:, s, :]).then_inc(sem(f"act_moe{l}"), 1)
            w("pe_moe", 4 * k + 2)
            nc.scalar.activation(sg[s][SLOT:P], ps[0:SLOT, 2 + s, :], ACT.Silu).then_inc(sem(f"act_moe{l}"), 1)
            w("pe_moe", 4 * k + 4)
            if not first:
                a.wait_ge(sem(f"sent{s}_{l}"), 16 * u)
            nc.scalar.copy(yo[s][0:SLOT, 0:512], ps[0:SLOT, 6 + s, :]).then_inc(sem(f"act_moe{l}"), 1)

        def expert_dve(v, l, k, u, s, first):
            w = waits(v, l)
            w("act_moe", 3 * k + 2)
            nc.vector.tensor_tensor(hid[s][0:SLOT], ps[SLOT:P, 2 + s, :], sg[s][SLOT:P], ALU.mult).then_inc(sem(f"dve_moe{l}"), 1)
            w("pe_moe", 4 * k + 3)
            nc.vector.tensor_copy(hidT[s].rearrange("p a b -> p (a b)"), ps[:, 4 + s, 0:4 * SLOT]).then_inc(sem(f"dve_moe{l}"), 1)
            w("pe_moe", 4 * k + 4)
            if not first:
                v.wait_ge(sem(f"sent{s}_{l}"), 16 * u)
            nc.vector.tensor_copy(yo[s][0:SLOT, 512:D], ps[SLOT:P, 6 + s, :]).then_inc(sem(f"dve_moe{l}"), 1)

        def pool_carry(pool, l, count):
            pool.wait_ge(sem(f"pool_moe{l}"), count)
            nc.gpsimd.tensor_tensor(carry, iota16[0:1, 0:1], iota16[0:1, 0:1], ALU.add).then_inc(sem(f"pool_moe{l}"), 1)

        def expert_gather(pool, l, k, q, s, first):
            if not first:
                waits(pool, l)("pe_moe", 4 * k - 7)
            pool.wait_ge(*dv.at(f"n{2 * l}gidx"))
            nc.gpsimd.tensor_copy(icol[0:SLOT, 0, s:s + 1], gidx[0:SLOT, bass.ds(k, 1)]).then_inc(sem(f"pool_moe{l}"), 1)
            pool_carry(pool, l, 1 + 2 * s if first else 8 * q + 5 + 2 * s)
            pool.indirect_dma_start(xg[s][0:SLOT], None, x_dram[l], bass.IndirectOffsetOnAxis(ap=icol[0:SLOT, 0, s:s + 1].bitcast(U32), axis=0),
                                    bounds_check=T - 1, oob_is_err=False).then_inc(sem(f"xg{s}_{l}"), 16)

        def expert_scatter(pool, l, k, q, s, first):
            if not first:
                pool.wait_ge(sem(f"sent{s}_{l}"), 16 * q)
            waits(pool, l)("act_moe", 3 * k + 3)
            waits(pool, l)("dve_moe", 3 * k + 3)
            nc.gpsimd.tensor_copy(icol[0:SLOT, 1, s:s + 1], lst[0:SLOT, bass.ds(k, 1)]).then_inc(sem(f"pool_moe{l}"), 1)
            pool_carry(pool, l, 8 * q + 9 + 2 * s)
            pool.indirect_dma_start(y_dram[l], bass.IndirectOffsetOnAxis(ap=icol[0:SLOT, 1, s:s + 1].bitcast(U32), axis=0), yo[s][0:SLOT], None,
                                    bounds_check=2 * T - 1, oob_is_err=False).then_inc(sem(f"sent{s}_{l}"), 16)

        PAIRS = NE // 2

        def expert_rounds(eng, body):
            for s in range(2):
                body(s, s, 0, s, True)
            with eng.Fori(1, PAIRS) as q:
                for s in range(2):
                    body(2 * q + s, 2 * q + s, q, s, False)

        def further_rounds(eng, body):
            with eng.Fori(1, ROUNDS) as r:
                with eng.Fori(0, PAIRS) as q:
                    for s in range(2):
                        body(NE * r + 2 * q + s, 2 * q + s, PAIRS * r + q, s, False)

        def if_crowded(eng, tag):
            eng.wait_ge(*dv.at(f"{tag}cnt"))
            return eng.If(eng.value_load(cnt[0:1, 1:2].bitcast(I32), min_val=0, max_val=T) > SLOT)

        def pool_pair(pool, l, k0, q, first=False):
            for s in range(2):
                expert_gather(pool, l, k0 + 2 + s, q, s, False)
            for s in range(2):
                expert_scatter(pool, l, k0 + s, q, s, first)

        def moe_pool(pool, tag, l):
            for s in range(2):
                nc.gpsimd.memset(xg[s], 0.0).then_inc(*po.done(f"{tag}xg_zero"))
            route_pool(pool, tag, l)
            pool.wait_ge(*po.at(f"{tag}xg_zero"))
            pool.wait_ge(*dv.at(f"{tag}gidx"))
            pool.wait_ge(sem(f"x_rows{l}"), 48)
            for s in range(2):
                expert_gather(pool, l, s, 0, s, True)
            pool_pair(pool, l, 0, 0, True)
            with pool.Fori(1, PAIRS) as q:
                pool_pair(pool, l, 2 * q, q)
            for s in range(2):
                pool.wait_ge(sem(f"sent{s}_{l}"), 16 * PAIRS)
                pool.wait_ge(sem(f"xg{s}_{l}"), 16 * PAIRS + 16)
            with if_crowded(pool, tag):
                with pool.Fori(1, ROUNDS) as r:
                    with pool.Fori(0, PAIRS) as q:
                        pool_pair(pool, l, NE * r + 2 * q, PAIRS * r + q)
                for s in range(2):
                    pool.wait_ge(sem(f"sent{s}_{l}"), 16 * PAIRS * ROUNDS)
                    pool.wait_ge(sem(f"xg{s}_{l}"), 16 * PAIRS * ROUNDS + 16)
            nc.gpsimd.memset(icol[0:1, 0, 0:1], 0).then_inc(*po.done(f"{tag}scattered"))

        def moe_engine(eng, tag, l, body):
            expert_rounds(eng, lambda k, e, u, s, first: body(eng, l, k, u, s, first))
            with if_crowded(eng, tag):
                further_rounds(eng, lambda k, e, u, s, first: body(eng, l, k, u, s, first))

        def moe_weights(q, tag, l):
            expert_rounds(q, lambda k, e, u, s, first: expert_weights(q, l, k, e, u, s, first))
            with if_crowded(q, tag):
                further_rounds(q, lambda k, e, u, s, first: expert_weights(q, l, k, e, u, s, first))

        def moe_result_load(q, tag, l):
            q.wait_ge(*po.at(f"{tag}scattered"))
            for i in range(3):
                q.dma_start(ybuf[0:tok(i), i], y_dram[l][2 * i * P:2 * (i * P + tok(i))].rearrange("(p j) d -> p j d", j=2)).then_inc(sem("y_in"), 16)

        def moe_act_scale(a, tag, l):
            a.wait_ge(sem(f"x_rows{l}"), 48)
            for i in range(3):
                a.wait_ge(*pe.at(f"{tag}xT7"))
                nc.scalar.mul(xres[0:tok(i), i], xres[0:tok(i), i], ALPHA).then_inc(*ac.done(f"{tag}alpha"))

        def moe_add(v, tag, l):
            def add(i, n):
                v.wait_ge(sem("y_in"), 48 * (l + 1))
                v.wait_ge(*ac.at(f"{tag}alpha"))
                for j in range(2):
                    nc.vector.scalar_tensor_tensor(xres[0:n, i], ybuf[0:n, i, j], comb[0:n, j, i:i + 1], xres[0:n, i], ALU.mult, ALU.add).then_inc(*dv.done())
                    if j == 0:
                        v.wait_ge(*dv.last())
            return add

        K1 = carve(work, A["raw"], bbT=DC * 2 * P, abh=2 * PT * NS, pcol=8 * PT)
        assert K1["end"] <= A["cv"] and M["end"] + 2048 <= lnp_at, (K1["end"], M["end"], lnp_at)
        bbT = view(work, K1["bbT"], DC, 2, P)
        CT = view(work, M["end"], DC, 2, P)
        abh = view(work, K1["abh"], 2, NS, PT)
        pcol = view(work, K1["pcol"], 8, PT)
        V = carve(work, M["ybuf"], B=2 * 512, C=2 * 512, h0=512, T=1024, bbD=2048)
        assert V["end"] <= M["xg"] and M["yo"] + 2048 <= M["route"]
        Bn = view(work, V["B"], 2, PT, C5)
        Cn = view(work, V["C"], 2, DC, N5)
        h0n = view(work, V["h0"], 2, 2, P)
        T5 = view(work, V["T"], 2, PT, C5)
        T8 = view(work, V["T"], 4, NS, PT)
        bbD = view(work, V["bbD"], 2, PT, 2, C5)
        CD = view(work, M["yo"], 2, DC, 2, N5)
        odd = view(work, M["hidT"], 2)
        par_i = view(work, M["hidT"] + 2, 2).bitcast(I32)

        def s5_matrix_loads(q):
            q.wait_ge(sem("cols_out"), 16)
            q.dma_start(pcol.rearrange("p a b -> p (a b)"), cols_dram).then_inc(sem("s5_cols_in"), 16)
            for i, n in enumerate(("re", "im")):
                q.dma_start(Bn[:, i], io[f"s5_B_{n}"].rearrange("o (t a) p c -> (o a p) t c", a=2)).then_inc(sem("s5_B_in"), 16)
                q.dma_start(Cn[:, i], io[f"s5_C_{n}"].rearrange("o (q g) c p -> (o g c) q p", q=DC)).then_inc(sem("s5_C_in"), 16)
                for b in range(NS):
                    q.dma_start(h0n[PT * (b % 4):PT * (b % 4 + 1), i, b // 4],
                                io[f"state_s5_{n}"][b].rearrange("o (t a) n -> (o t) (a n)", a=2)).then_inc(sem("s5_h0_in"), 16)

        def s5_matrix_pool(pool):
            pool.wait_ge(*pe.at("mixAB2"))
            nc.gpsimd.memset(bbD, 0.0).then_inc(*po.done("bbD_zero"))

        def s5_matrix_dve(v):
            per_c = lambda i: pcol[:, i].unsqueeze(2).to_broadcast([P, PT, C5])
            per_b = lambda i: pcol[:, i].unsqueeze(1).to_broadcast([P, NS, PT])
            (ABR, ABI, ZR, ZI) = (3, 4, 5, 6)
            tt = lambda o, a, b, op, name=None: nc.vector.tensor_tensor(o, a, b, op).then_inc(*dv.done(name))
            v.wait_ge(sem("s5_cols_in"), 16)
            v.wait_ge(sem("s5_B_in"), 32)
            v.wait_ge(*po.at("bbD_zero"))
            for w, (x, y, op) in enumerate(((0, 1, ALU.subtract), (1, 0, ALU.add))):
                tt(T5[:, 0], Bn[:, x], per_c(ZR), ALU.mult)
                tt(T5[:, 1], Bn[:, y], per_c(ZI), ALU.mult)
                v.wait_ge(*dv.last())
                for g in range(2):
                    at = slice(g * N5, (g + 1) * N5)
                    tt(bbD[at, w, :, g], T5[at, 0], T5[at, 1], op, "bbD")
                v.wait_ge(*dv.last())
            nc.vector.tensor_single_scalar(par_i[:, 0:1], value[:, 0, 0:1], 5, ALU.logical_shift_right).then_inc(*dv.done())
            v.wait_ge(*dv.last())
            nc.vector.tensor_single_scalar(par_i[:, 1:2], par_i[:, 0:1], 1, ALU.bitwise_and).then_inc(*dv.done())
            v.wait_ge(*dv.last())
            nc.vector.tensor_copy(odd[:, 1:2], par_i[:, 1:2]).then_inc(*dv.done())
            v.wait_ge(*dv.last())
            nc.vector.tensor_scalar(odd[:, 0:1], odd[:, 1:2], -1.0, 1.0, ALU.mult, ALU.add).then_inc(*dv.done())
            v.wait_ge(*dv.last())
            v.wait_ge(sem("s5_C_in"), 32)
            for w in range(2):
                for g in range(2):
                    nc.vector.tensor_scalar(CD[:, w, :, g], Cn[:, w], odd[:, g:g + 1], None, ALU.mult).then_inc(*dv.done("CD"))
            v.wait_ge(*pe.at("h0T"))
            h0 = ps[:, 7, :].rearrange("p (w b t) -> p w b t", w=2, b=NS)
            for i, (x, y) in enumerate(((0, ABR), (1, ABI), (1, ABR), (0, ABI))):
                tt(T8[:, i], h0[:, x], per_b(y), ALU.mult)
            v.wait_ge(*dv.last())
            tt(abh[:, 0], T8[:, 0], T8[:, 1], ALU.subtract)
            tt(abh[:, 1], T8[:, 2], T8[:, 3], ALU.add, "abh")

        def s5_matrix_pe(t):
            t.wait_ge(sem("s5_h0_in"), 16 * 2 * NS)
            for w in range(2):
                for h in range(2):
                    last = nc.tensor.transpose(ps[:, 7, (2 * w + h) * P:(2 * w + h + 1) * P], h0n[:, w, h], ident)
            last.then_inc(*pe.done("h0T"))
            for name, src, need in (("bbT", bbD, "bbD"), ("CT", CD, "CD")):
                t.wait_ge(*dv.at(need))
                flat_src = src.rearrange("p w t g c -> p w (t g c)")
                for q in range(DC):
                    if name == "CT" and q % 2 == 0:
                        t.wait_ge(*ac.at(f"bbT{q // 2}"))
                    for w in range(2):
                        last = nc.tensor.transpose(ps[:, 2 + q // 2, ((q % 2) * 2 + w) * P:((q % 2) * 2 + w + 1) * P],
                                                   flat_src[:, w, q * P:(q + 1) * P], ident)
                    if q % 2:
                        last.then_inc(*pe.done(f"{name}{q // 2}"))

        def s5_matrix_act(a):
            for name, dst in (("bbT", bbT), ("CT", CT)):
                for j in range(4):
                    a.wait_ge(*pe.at(f"{name}{j}"))
                    nc.scalar.copy(dst[:, 2 * j:2 * j + 2].rearrange("p a b c -> p (a b c)"), ps[:, 2 + j, :]).then_inc(*ac.done(f"{name}{j}"))

        NPAIR = PT // 2
        L5 = carve(work, M["mix"], gyT=DC * T, hs=2 * PT * NS, hl=2 * PT, tab=4 * 1024, a=2 * 2048, mat=2 * 640,
                   hout=6 * P, mag=10, u=2 * T, hslot=4 * 4 * NS)
        assert L5["end"] <= M["end"], (L5["end"], M["end"])
        gyT = view(work, L5["gyT"], DC, T)
        hs_all = view(work, L5["hs"], 2, NS, PT)
        hlast = view(work, L5["hl"], 2, PT)
        tab = [view(work, L5["tab"] + s * 1024, 2, 2, SEQ) for s in range(4)]
        aa = [view(work, L5["a"] + s * 2048, 4, 2, SEQ) for s in range(2)]
        pp = [view(ring, 20480 + s * 2048, 4, 2, SEQ) for s in range(2)]
        mat_b = [view(work, L5["mat"] + s * 640, 2, P) for s in range(2)]
        mat_c = [view(work, L5["mat"] + s * 640 + 256, 3, P) for s in range(2)]
        mag = [view(work, L5["mag"] + 5 * c, 4) for c in range(2)]
        dcol = [view(work, L5["mag"] + 5 * c + 4, 1) for c in range(2)]
        ucol = [view(work, L5["u"] + c * T, T) for c in range(2)]
        hslot = [view(work, L5["hslot"] + s * 4 * NS, 2, NS, 2) for s in range(4)]
        hout = view(work, L5["hout"], 6, P)
        glu_w = [view(ring, i * 8192, DC, D) for i in range(2)]
        sig = view(work, L5["tab"], 2, D)
        prod = view(work, L5["a"], 2, D)

        def s5_slot_loads(sp):
            def load(j, s, first):
                if not first:
                    sp.wait_ge(sem("s5_last"), 3 * j - 9)
                sp.dma_start(tab[s].rearrange("p w t n -> p (w t n)").unsqueeze(1), F_dram.rearrange("j p w t n -> p j (w t n)")[:, bass.ds(j, 1)]).then_inc(sem(f"tab_in{s}"), 16)
            sp.wait_ge(*dv.at("n1mv2"))
            for s in range(4):
                load(s, s, True)
            with sp.Fori(1, NPAIR // 4) as u:
                for s in range(4):
                    load(4 * u + s, s, False)

        def s5_bu(t, j, q, c, s, u, first):
            t.wait_ge(sem("s5_b"), 2 * q + 2)
            if not first:
                t.wait_ge(sem("s5_pre"), 5 * j)
            for i in range(2):
                rows = slice((2 * s + i) * 32, (2 * s + i + 1) * 32)
                for w in range(2):
                    nc.tensor.matmul(ps[:, 2 * s + i, w * SEQ:(w + 1) * SEQ], mat_b[c][rows, w], ucol[c][rows, 0:SEQ],
                                     start=True, stop=True)
                    last = nc.tensor.matmul(ps[:, 6 + i, w * NS:(w + 1) * NS], mat_b[c][rows, w],
                                            ucol[c][rows, SEQ:], start=True, stop=True)
            last.then_inc(sem("s5_bu"), 1)

        def s5_y(t, j, q, c, s, first):
            t.wait_ge(sem("s5_c"), 4 * q + 4)
            t.wait_ge(sem("s5_post_v"), 2 * j + 2)
            t.wait_ge(sem("s5_post_p"), 2 * j + 2)
            if not first and s == 0:
                t.wait_ge(sem("s5_yd"), q - 1)
            for i in range(2):
                at = (2 * s + i) * 32
                o = ps[at:at + 32, 4 + c, 0:SEQ]
                for n, (m, x) in enumerate(((0, 0), (1, 1), (2, 2), (2, 3))):
                    nc.tensor.matmul(o, mat_c[c][:, m, at:at + 32], pp[s][:, x, i], start=n == 0, stop=n == 3)
                o = ps[at:at + 32, 4 + c, SEQ:T]
                for n, (m, w) in enumerate(((0, 0), (2, 1))):
                    last = nc.tensor.matmul(o, mat_c[c][:, m, at:at + 32], hslot[2 * c + s][:, w, :, i],
                                            start=n == 0, stop=n == 1)
            last.then_inc(sem("s5_y"), 1)

        def s5_pe(t):
            for tag in ("n1",):
                t.wait_ge(*ac.at(f"{tag}xT"))
                t.wait_ge(*dv.at(f"{tag}xT"))
            for s in range(2):
                s5_bu(t, s, 0, 0, s, 0, s == 0)
            def chunk(q, c, first, more):
                for s in range(2):
                    if more:
                        s5_bu(t, 2 * q + 2 + s, q + 1, 1 - c, s, None, False)
                    s5_y(t, 2 * q + s, q, c, s, first)
            for c in range(2):
                chunk(c, c, True, True)
            with t.Fori(1, DC // 2 - 1) as i:
                for c in range(2):
                    chunk(2 * i + c, c, False, True)
            chunk(DC - 2, 0, False, True)
            chunk(DC - 1, 1, False, False)

        def s5_pre(v, j, u, c, s, first, deep):
            v.wait_ge(sem("s5_bu"), j + 1)
            v.wait_ge(sem(f"tab_in{2 * c + s}"), 16 * u + 16)
            if not first:
                v.wait_ge(sem("s5_post_v"), 2 * j - 2)
                v.wait_ge(sem("s5_post_p"), 2 * j - 2)
            if deep:
                v.wait_ge(sem("s5_y"), j - 3)
                v.wait_ge(sem("s5_last"), 3 * j - 9)
            re, im = (ps[:, 2 * s:2 * s + 2, w * SEQ:(w + 1) * SEQ] for w in range(2))
            for n, (x, w) in enumerate(((re, 0), (im, 1), (im, 0), (re, 1))):
                nc.vector.tensor_tensor(aa[s][:, n], x, tab[2 * c + s][:, w], ALU.mult).then_inc(sem("s5_pre"), 1)
            nc.vector.tensor_tensor(hslot[2 * c + s], ps[:, 6:8, 0:2 * NS].rearrange("p a (w b) -> p w b a", w=2),
                                    abh[:, :, :, bass.ds(2 * j, 2)], ALU.add).then_inc(sem("s5_pre"), 1)

        def s5_scan(v, j, q, c, s, first):
            v.wait_ge(sem("s5_add"), 2 * j + 2)
            v.wait_ge(sem("s5_c"), 4 * (q + 1))
            for w in range(2):
                for i in range(2):
                    nc.vector.tensor_tensor_scan(aa[s][:, 2 * w + 1, i], mag[c][:, 2 * s + i:2 * s + i + 1].to_broadcast([P, SEQ]), aa[s][:, 2 * w, i],
                                                 0.0, ALU.mult, ALU.add).then_inc(sem("s5_scan"), 1)
            v.wait_ge(sem("s5_scan"), 4 * j + 4)
            if not first:
                v.wait_ge(sem("s5_y"), j - 1)
            for n in (0, 1):
                nc.vector.tensor_tensor(pp[s][:, 2 * n], aa[s][:, 1], tab[2 * c + s][:, n], ALU.mult).then_inc(sem("s5_post_v"), 1)

        def s5_skip(v, q, c, first):
            v.wait_ge(sem("s5_y"), 2 * q + 2)
            chunk_of = lambda x: x[:, bass.ds(q, 1)].rearrange("p a b -> p (a b)")
            nc.vector.scalar_tensor_tensor(chunk_of(gyT), chunk_of(xT), dcol[c], ps[:, 4 + c, 0:T],
                                           ALU.mult, ALU.add).then_inc(sem("s5_yd"), 1)

        def s5_dve(v):
            v.wait_ge(*dv.last())
            s5_pre(v, 0, 0, 0, 0, True, False)

            def chunk(q, c, u, first, more, skip, deep=True):
                for s in range(2):
                    if s == 0:
                        s5_pre(v, 2 * q + 1, u, c, 1, first, deep)
                        if skip is not None:
                            s5_skip(v, q - 1, 1 - c, skip)
                    elif more:
                        s5_pre(v, 2 * q + 2, u + c, 1 - c, 0, False, deep or c == 1)
                    s5_scan(v, 2 * q + s, q, c, s, first)
            chunk(0, 0, 0, True, True, None, False)
            chunk(1, 1, 0, False, True, True, False)
            chunk(2, 0, 1, False, True, True)
            with v.Fori(1, DC // 2 - 1) as i:
                for c in range(2):
                    chunk(2 * i + 1 + c, 1 - c, i + c, False, True, False)
            chunk(DC - 1, 1, DC // 2 - 1, False, False, False)
            s5_skip(v, DC - 1, 1, False)

        def s5_add(pool, j, s, first):
            pool.wait_ge(sem("s5_pre"), 5 * j + 5)
            nc.gpsimd.tensor_tensor(aa[s][:, 0], aa[s][:, 0], aa[s][:, 1], ALU.add).then_inc(sem("s5_add"), 1)
            nc.gpsimd.tensor_tensor(aa[s][:, 2], aa[s][:, 2], aa[s][:, 3], ALU.subtract).then_inc(sem("s5_add"), 1)

        def s5_post(pool, j, c, s, first):
            pool.wait_ge(sem("s5_scan"), 4 * j + 4)
            if not first:
                pool.wait_ge(sem("s5_y"), j - 1)
                pool.wait_ge(sem("s5_last"), 3 * j - 3)
            for n, w in ((1, 1), (3, 0)):
                nc.gpsimd.tensor_tensor(pp[s][:, n], aa[s][:, 3], tab[2 * c + s][:, w], ALU.mult).then_inc(sem("s5_post_p"), 1)
            pool.wait_ge(sem("s5_post_p"), 2 * j + 2)
            pool.wait_ge(sem("s5_post_v"), 2 * j + 2)
            end = lambda x: pp[s][:, x, :, SEQ - 1:SEQ].rearrange("p a b -> p (a b)")
            for w, (x, y, op) in enumerate(((0, 1, ALU.subtract), (2, 3, ALU.add))):
                nc.gpsimd.tensor_tensor(hlast[:, w, bass.ds(2 * j, 2)], end(x), end(y), op).then_inc(sem("s5_last"), 1)
            nc.gpsimd.tensor_copy(hs_all[:, :, :, bass.ds(2 * j, 2)], hslot[2 * c + s]).then_inc(sem("s5_last"), 1)

        def s5_pool(pool):
            s5_add(pool, 0, 0, True)
            def four(j0, first, more):
                for k in range(4):
                    s5_post(pool, j0 + k, k // 2, k % 2, first and k < 2)
                    if more or k < 3:
                        s5_add(pool, j0 + k + 1, 1 - k % 2, False)
            four(0, True, True)
            with pool.Fori(1, NPAIR // 4 - 1) as u:
                four(4 * u, False, True)
            four(NPAIR - 4, False, False)

        def s5_mats(a, q, c, first):
            if not first:
                a.wait_ge(sem("s5_bu"), 2 * q - 2)
            nc.scalar.copy(mat_b[c], bbT[:, bass.ds(q, 1)].rearrange("p q a b -> p (q a) b")).then_inc(sem("s5_b"), 1)
            nc.scalar.copy(ucol[c].unsqueeze(1), xT[:, bass.ds(q, 1)]).then_inc(sem("s5_b"), 1)
            if not first:
                a.wait_ge(sem("s5_y"), 2 * q - 2)
                a.wait_ge(sem("s5_yd"), q - 1)
            src = CT[:, bass.ds(q, 1)].rearrange("p q a b -> p (q a) b")
            nc.scalar.copy(mat_c[c][:, 0], src[:, 0]).then_inc(sem("s5_c"), 1)
            nc.scalar.mul(mat_c[c][:, 1:3], src, -1.0).then_inc(sem("s5_c"), 1)
            nc.scalar.copy(dcol[c], pcol[:, 7, bass.ds(q, 1)]).then_inc(sem("s5_c"), 1)
            nc.scalar.copy(mag[c], pcol[:, 2, bass.ds(4 * q, 4)]).then_inc(sem("s5_c"), 1)

        def s5_act(a):
            a.wait_ge(*ac.at("n1xT"))
            a.wait_ge(*dv.at("n1xT"))
            for c in range(2):
                s5_mats(a, c, c, True)
            with a.Fori(1, DC // 2) as i:
                for c in range(2):
                    s5_mats(a, 2 * i + c, c, False)

        def s5_gelu(a):
            a.wait_ge(sem("s5_yd"), DC)
            nc.scalar.activation(gyT, gyT, ACT.Gelu_apprx_tanh).then_inc(*ac.done("gelu"))

        def s5_state_pe(t):
            t.wait_ge(sem("s5_last"), 3 * NPAIR)
            t.wait_ge(sem("s5_pre"), 5 * NPAIR)
            for w in range(2):
                for h in range(2):
                    nc.tensor.transpose(ps[:, 0, (2 * w + h) * P:(2 * w + h + 1) * P],
                                        hs_all[:, w, 4 * h:4 * h + 4].rearrange("p a b -> p (a b)"), ident)
                last = nc.tensor.transpose(ps[0:PT, 1, w * P:(w + 1) * P], hlast[:, w], ident)
            last.then_inc(*pe.done("s5_states"))

        def s5_state_act(a):
            a.wait_ge(*pe.at("s5_states"))
            nc.scalar.copy(hout[:, 0:4].rearrange("p a b -> p (a b)"), ps[:, 0, :]).then_inc(*ac.done())
            nc.scalar.copy(hout[0:PT, 4:6].rearrange("p a b -> p (a b)"), ps[0:PT, 1, 0:2 * P]).then_inc(*ac.done("s5_states"))

        def s5_state_stores(q):
            q.wait_ge(*ac.at("s5_states"))
            for w, n in enumerate(("re", "im")):
                for b in range(NS):
                    q.dma_start(out[f"s_{n}"][b].rearrange("o (t a) n -> (o t) (a n)", a=2),
                                hout[PT * (b % 4):PT * (b % 4 + 1), 2 * w + b // 4]).then_inc(sem("stores_s5"), 16)
                q.dma_start(out[f"p_{n}"].rearrange("x o (t a) n -> (x o t) (a n)", a=2), hout[0:PT, 4 + w]).then_inc(sem("stores_s5"), 16)

        def glu_loads(q):
            q.wait_ge(*pe.at("n1xT7"))
            for i, n in enumerate("ab"):
                q.dma_start(glu_w[i], io[f"s5_w_glu_{n}"].rearrange("o (k p) n -> p (o k) n", p=P)).then_inc(sem("glu_in"), 16)

        def glu_pe(t):
            t.wait_ge(*ac.at("gelu"))
            t.wait_ge(sem("glu_in"), 32)
            t.wait_ge(*ac.at("s5_states"))
            for i in range(TT):
                for k in range(DC):
                    for b in range(4):
                        last = nc.tensor.matmul(ps[:, 4 * i + b, :], gyT[:, k, i * P:(i + 1) * P], glu_w[b // 2][:, k, (b % 2) * 512:(b % 2 + 1) * 512],
                                                start=k == 0, stop=k == DC - 1)
                last.then_inc(*pe.done(f"glu{i}"))
            t.wait_ge(*dv.at("prod0"))
            for k in range(DC):
                for b in range(4):
                    last = nc.tensor.matmul(ps[32 * b:32 * b + NS, 0, :], gyT[:, k, SEQ:], glu_w[b // 2][:, k, (b % 2) * 512:(b % 2 + 1) * 512],
                                            start=k == 0, stop=k == DC - 1)
            last.then_inc(*pe.done("glu2"))

        def glu_act(a):
            for i in range(TT):
                a.wait_ge(*pe.at(f"glu{i}"))
                nc.scalar.activation(sig[:, i], banks(4 * i + 2, 2), ACT.Tanh, scale=0.5).then_inc(*ac.done(f"tanh{i}"))
            a.wait_ge(*pe.at("glu2"))
            a.wait_ge(*dv.at("prod0"))
            for h in range(2):
                nc.scalar.activation(sig[0:NS, 0, h * 512:(h + 1) * 512], ps[64 + 32 * h:64 + 32 * h + NS, 0, :], ACT.Tanh, scale=0.5).then_inc(*ac.done("tanh2"))

        def glu_add(v):
            def add(i, n):
                v.wait_ge(*ac.at(f"tanh{i}"))
                v.wait_ge(*ac.at("alpha_s5"))
                s = i % 2
                if i < TT:
                    nc.vector.scalar_tensor_tensor(prod[:, s], sig[:, s], 1.0, banks(4 * i, 2), ALU.add, ALU.mult).then_inc(*dv.done(f"prod{i}"))
                else:
                    v.wait_ge(*dv.last())
                    for h in range(2):
                        at = slice(h * 512, (h + 1) * 512)
                        nc.vector.scalar_tensor_tensor(prod[0:n, s, at], sig[0:n, s, at], 1.0, ps[32 * h:32 * h + n, 0, :], ALU.add, ALU.mult).then_inc(*dv.done())
                v.wait_ge(*dv.last())
                nc.vector.scalar_tensor_tensor(xres[0:n, i], prod[0:n, s], 0.5, xres[0:n, i], ALU.mult, ALU.add).then_inc(*dv.done())
            return add

        def scale_residual(a):
            a.wait_ge(*pe.at("n1xT7"))
            for i in range(3):
                nc.scalar.mul(xres[0:tok(i), i], xres[0:tok(i), i], ALPHA).then_inc(*ac.done("alpha_s5"))

        block = ctx.enter_context(nc.Block())

        @block.sync
        def _(sp):
            ab_loads(sp)
            ab_stores(sp)
            sp.wait_ge(*dv.at("s_final"))
            sp.dma_start(xtok[:, 0:TT, :], x_all[0]).then_inc(sem("x_again"), 16)
            sp.dma_start(xtok[0:NS, TT, :], x_all[1]).then_inc(sem("x_again"), 16)
            ln_load(sp, "ln_mix_g", "ln_mix_b", 0, None)
            sp.wait_ge(sem("stores_C"), 64)
            sp.wait_ge(*pe.at("mixAB2"))
            s5_matrix_loads(sp)
            moe_weights(sp, "n0", 0)
            s5_slot_loads(sp)
            glu_loads(sp)
            s5_state_stores(sp)
            sp.wait_ge(*pe.at("glu2"))
            moe_weights(sp, "n2", 1)
            for i in range(3):
                sp.wait_ge(*po.at(f"n3x{i}"))
                dst = out["y_p"].rearrange("o (t p) d -> p (o t) d", p=P)[:, i] if i < TT else out["y_s"].rearrange("b o d -> (b o) d")
                sp.dma_start(dst, xres[0:tok(i), i]).then_inc(sem("stores_y"), 16)
            sp.wait_ge(sem("stores_y"), 48)
            sp.wait_ge(sem("stores_s5"), 16 * 2 * (NS + 1))
            sp.wait_ge(sem("stores"), 16 * (1 + 2 + 4 + 1 + 4 + 1))
            sp.wait_ge(sem("stores_S"), 16)
            sp.wait_ge(sem("stores_conv"), 32)

        @block.gpsimd
        def _(pool):
            ab_consts(pool)
            moe_consts_pool(pool)
            s5_param_pool(pool)
            s5_tables_pool(pool)
            gdn_pool(pool)
            ml_pool(pool)
            ln_pool(pool, "n0")
            s5_matrix_pool(pool)
            moe_pool(pool, "n0", 0)
            ln_pool(pool, "n1")
            s5_pool(pool)
            ln_pool(pool, "n2")
            moe_pool(pool, "n2", 1)
            ln_pool(pool, "n3")

        @block.scalar
        def _(act):
            ab_small_loads(act)
            moe_consts_loads(act)
            ab_act_project(act)
            gdn_act(act)
            ml_act(act)
            ln_act(act, "n0")
            xT_copy(act, ac, nc.scalar.copy, "n0", 0)
            route_loads(act, "n0", 0)
            route_act(act, "n0")
            s5_matrix_act(act)
            moe_act_scale(act, "n0", 0)
            moe_engine(act, "n0", 0, expert_act)
            moe_result_load(act, "n0", 0)
            ln_load(act, "ln_ffn_g", "ln_ffn_b", 0, po.at("n0x2"))
            ln_act(act, "n1")
            xT_copy(act, ac, nc.scalar.copy, "n1", 0)
            scale_residual(act)
            ln_load(act, "ln_mix_g", "ln_mix_b", 1, po.at("n1x2"))
            s5_act(act)
            s5_gelu(act)
            s5_state_act(act)
            glu_act(act)
            ln_act(act, "n2")
            xT_copy(act, ac, nc.scalar.copy, "n2", 0)
            route_loads(act, "n2", 1)
            route_act(act, "n2")
            moe_act_scale(act, "n2", 1)
            moe_engine(act, "n2", 1, expert_act)
            moe_result_load(act, "n2", 1)
            ln_load(act, "ln_ffn_g", "ln_ffn_b", 1, po.at("n2x2"))
            ln_act(act, "n3")

        @block.vector
        def _(dve):
            ab_dve_project(dve)
            gdn_dve(dve)
            ml_dve(dve)

            def add_ab(i, n):
                dve.wait_ge(sem("x_again"), 32)
                dve.wait_ge(*pe.at(f"mixAB{i}"))
                if i < TT:
                    nc.vector.scalar_tensor_tensor(xres[:, i], xres[:, i], ALPHA, banks(2 * i, 2), ALU.mult, ALU.add).then_inc(*dv.done(f"add_ab{i}"))
                    return
                for h in range(2):
                    at = slice(h * 512, (h + 1) * 512)
                    nc.vector.scalar_tensor_tensor(xres[0:n, i, at], xres[0:n, i, at], ALPHA, ps[64 * h:64 * h + n, 4, :], ALU.mult, ALU.add).then_inc(*dv.done(f"add_ab{i}"))
            ln_dve(dve, "n0", 1, add_ab)
            xT_copy(dve, dv, nc.vector.tensor_copy, "n0", 1)
            route_dve(dve, "n0")
            s5_matrix_dve(dve)
            route_lists(dve, "n0")
            moe_engine(dve, "n0", 0, expert_dve)
            ln_dve(dve, "n1", 2, moe_add(dve, "n0", 0))
            xT_copy(dve, dv, nc.vector.tensor_copy, "n1", 1)
            s5_dve(dve)
            ln_dve(dve, "n2", 3, glu_add(dve))
            xT_copy(dve, dv, nc.vector.tensor_copy, "n2", 1)
            dve.wait_ge(sem("stores_s5"), 16 * 2 * (NS + 1))
            route_dve(dve, "n2")
            route_lists(dve, "n2")
            moe_engine(dve, "n2", 1, expert_dve)
            ln_dve(dve, "n3", 4, moe_add(dve, "n2", 1))

        @block.tensor
        def _(te):
            ab_pe_project(te)
            gdn_pe(te)
            ml_pe(te)
            xT_pe(te, "n0", [])
            route_pe(te, "n0")
            s5_matrix_pe(te)
            te.wait_ge(*ac.at("CT3"))
            te.wait_ge(*dv.at("n0gidx"))
            moe_engine(te, "n0", 0, expert_pe)
            xT_pe(te, "n1", [])
            s5_pe(te)
            s5_state_pe(te)
            glu_pe(te)
            xT_pe(te, "n2", [ac.at("tanh2"), dv.at("n2mv2")])
            route_pe(te, "n2")
            te.wait_ge(*dv.at("n2gidx"))
            moe_engine(te, "n2", 1, expert_pe)


OUTS = (("y_p", (1, SEQ, D)), ("y_s", (NS, 1, D)),
        ("p_conv", (1, 1, CW - 1, CONV)), ("p_S", (1, 1, H, DK, DK)), ("p_C", (1, 1, H, DK, DK)), ("p_n", (1, 1, H, DK)),
        ("p_m", (1, 1, H)), ("p_re", (1, 1, G5, N5)), ("p_im", (1, 1, G5, N5)),
        ("s_conv", (NS, 1, CW - 1, CONV)), ("s_S", (NS, 1, H, DK, DK)), ("s_C", (NS, 1, H, DK, DK)), ("s_n", (NS, 1, H, DK)),
        ("s_m", (NS, 1, H)), ("s_re", (NS, 1, G5, N5)), ("s_im", (NS, 1, G5, N5)))


def kernel(**inputs):
    import concourse.bacc as bacc
    from concourse.bass_utils import run_bass_kernel_spmd

    arrays = {name: np.ascontiguousarray(a) for name, a in inputs.items()}
    book = {"known": {}, "new": {}}
    for _ in range(2):
        nc = bacc.Bacc("TRN2", target_bir_lowering=False, num_devices=1)
        io = {name: nc.dram_tensor(f"in_{name}", a.shape, mybir.dt.from_np(a.dtype), kind="ExternalInput").ap()
              for name, a in arrays.items()}
        out = {name: nc.dram_tensor(f"out_{name}", shape, F32, kind="ExternalOutput").ap() for name, shape in OUTS}
        build(nc, io, out, book)
        book = {"known": book["new"], "new": {}}
    r = run_bass_kernel_spmd(nc, [{f"in_{name}": a for name, a in arrays.items()}], core_ids=[0])
    return tuple(r.results[0][f"out_{name}"] for name, _ in OUTS)
```
